# Optimizing a Trainium2 kernel written in Bass

```python
import jax, jax.numpy as jnp
from jax import lax
import numpy as np

D_MODEL = 2048
BATCH = 1
SEQ = 256
DEPTH = 2

HEAD_DIM = 128
ROT_DIM = HEAD_DIM // 4
ROPE_THETA = 500000.0
NORM_EPS = 1e-6

DIL_GROUPS = ((128, 1), (512, 4), (2048, 16))
A_SLOTS = D_MODEL // 512
A_HEADS = A_SLOTS * len(DIL_GROUPS)
A_WIDTH = A_SLOTS * HEAD_DIM
B_Q_HEADS = D_MODEL // 256
B_KV_HEADS = B_Q_HEADS // 4
B_HALF_WINDOW = 128
B_WIDTH = B_Q_HEADS * HEAD_DIM
C_HEADS = D_MODEL // 256
C_DK = 128
C_DV = 128
C_WIDTH = C_HEADS * C_DV
C_CHUNK = 64
N_BRANCHES = 3

SPLIT_SIZES = (
    3 * A_HEADS * HEAD_DIM,
    A_WIDTH,
    B_Q_HEADS * HEAD_DIM,
    B_KV_HEADS * HEAD_DIM,
    B_KV_HEADS * HEAD_DIM,
    B_WIDTH,
    C_HEADS * C_DK,
    C_HEADS * C_DK,
    C_HEADS * C_DK,
    C_HEADS * C_DV,
    C_WIDTH,
    N_BRANCHES * D_MODEL,
)
IN_COLS = sum(SPLIT_SIZES)

kernel_name = "hybrid_dilated_window_hgrn2_encoder"

def rms_norm(t, gain):
    t32 = t.astype(jnp.float32)
    y = t32 * lax.rsqrt(jnp.mean(t32 * t32, axis=-1, keepdims=True) + NORM_EPS)
    return (y * gain.astype(jnp.float32)).astype(t.dtype)

def rope_tables(seq):
    pos = jnp.arange(seq, dtype=jnp.float32)
    inv_freq = ROPE_THETA ** (-jnp.arange(0, ROT_DIM, 2, dtype=jnp.float32) / ROT_DIM)
    ang = pos[:, None] * inv_freq[None, :]
    return jnp.cos(ang), jnp.sin(ang)

def apply_partial_rope(t, cos, sin):
    half = ROT_DIM // 2
    t32 = t.astype(jnp.float32)
    x1, x2, rest = t32[..., :half], t32[..., half:ROT_DIM], t32[..., ROT_DIM:]
    c, s = cos[:, None, :], sin[:, None, :]
    return jnp.concatenate([x1 * c - x2 * s, x2 * c + x1 * s, rest], axis=-1).astype(t.dtype)

def banded_window_attention(q, k, v, half_window, sink=None):
    bsz, L, hq, dh = q.shape
    hkv = k.shape[2]
    grp = hq // hkv
    blk = half_window
    nb = -(-L // blk)
    lp = nb * blk
    pad = lp - L
    q = jnp.pad(q, ((0, 0), (0, pad), (0, 0), (0, 0)))
    kpad = ((0, 0), (blk, pad + blk), (0, 0), (0, 0))
    k = jnp.pad(k, kpad)
    v = jnp.pad(v, kpad)

    def three_blocks(t):
        t = t.reshape(bsz, nb + 2, blk, hkv, dh)
        return jnp.concatenate([t[:, :-2], t[:, 1:-1], t[:, 2:]], axis=2)

    kb, vb = three_blocks(k), three_blocks(v)
    qb = q.reshape(bsz, nb, blk, hkv, grp, dh)
    s = jnp.einsum('bnqhgd,bnkhd->bnhgqk', qb, kb,
                   preferred_element_type=jnp.float32) * (dh ** -0.5)
    qpos = jnp.arange(lp).reshape(nb, blk)
    kpos = (jnp.arange(nb)[:, None] - 1) * blk + jnp.arange(3 * blk)[None, :]
    rel = kpos[:, None, :] - qpos[:, :, None]
    valid = (jnp.abs(rel) <= half_window) & (kpos[:, None, :] >= 0) & (kpos[:, None, :] < L)
    s = jnp.where(valid[None, :, None, None], s, -jnp.inf)
    m = jnp.max(s, axis=-1, keepdims=True)
    if sink is not None:
        sink_b = sink.astype(jnp.float32).reshape(1, 1, hkv, grp, 1, 1)
        m = jnp.maximum(m, sink_b)
    p = jnp.exp(s - m)
    denom = jnp.sum(p, axis=-1, keepdims=True)
    if sink is not None:
        denom = denom + jnp.exp(sink_b - m)
    o = jnp.einsum('bnhgqk,bnkhd->bnqhgd', p / denom, vb.astype(jnp.float32))
    lse = (m + jnp.log(denom))[..., 0].transpose(0, 1, 4, 2, 3)
    o = o.reshape(bsz, lp, hq, dh)[:, :L]
    lse = lse.reshape(bsz, lp, hq)[:, :L]
    return o, lse

def dilated_attention(q, k, v):
    bsz, s, _, dh = q.shape
    outs, lses = [], []
    for g, (window, dil) in enumerate(DIL_GROUPS):
        hs = slice(g * A_SLOTS, (g + 1) * A_SLOTS)

        def gather(t):
            t = t[:, :, hs].reshape(bsz, s // dil, dil, A_SLOTS, dh)
            return t.transpose(0, 2, 1, 3, 4).reshape(bsz * dil, s // dil, A_SLOTS, dh)

        o, lse = banded_window_attention(gather(q), gather(k), gather(v), window // (2 * dil))
        o = o.reshape(bsz, dil, s // dil, A_SLOTS, dh).transpose(0, 2, 1, 3, 4).reshape(bsz, s, A_SLOTS, dh)
        lse = lse.reshape(bsz, dil, s // dil, A_SLOTS).transpose(0, 2, 1, 3).reshape(bsz, s, A_SLOTS)
        outs.append(o)
        lses.append(lse)
    w = jax.nn.softmax(jnp.stack(lses), axis=0)
    out = jnp.einsum('gbsh,gbshd->bshd', w, jnp.stack(outs))
    return out.reshape(bsz, s, A_WIDTH)

def gla_chunk_scan(q, k, log_f, v):
    bsz, s, h, dk = q.shape
    dv = v.shape[-1]
    n = s // C_CHUNK

    def to_chunks(t):
        return t.reshape(bsz, n, C_CHUNK, h, t.shape[-1]).transpose(1, 0, 3, 2, 4)

    causal = jnp.tril(jnp.ones((C_CHUNK, C_CHUNK), dtype=bool))[:, :, None]

    def step(state, inp):
        qx, kx, lfx, vx = inp
        b = jnp.cumsum(lfx, axis=2)
        rel = b[:, :, :, None, :] - b[:, :, None, :, :]
        decay = jnp.exp(jnp.where(causal, rel, -jnp.inf))
        scores = jnp.einsum('bhtk,bhsk,bhtsk->bhts', qx, kx, decay)
        o = (jnp.einsum('bhts,bhsv->bhtv', scores, vx)
             + jnp.einsum('bhtk,bhkv->bhtv', qx * jnp.exp(b), state))
        b_last = b[:, :, -1:, :]
        state = (state * jnp.exp(b_last)[:, :, 0, :, None]
                 + jnp.einsum('bhsk,bhsv->bhkv', kx * jnp.exp(b_last - b), vx))
        return state, o

    state0 = jnp.zeros((bsz, h, dk, dv), jnp.float32)
    _, o = lax.scan(step, state0, (to_chunks(q), to_chunks(k), to_chunks(log_f), to_chunks(v)))
    return o.transpose(1, 0, 3, 2, 4).reshape(bsz, s, h, dv)

def hgrn2_bidirectional(q, f_fwd, f_bwd, inp, gate, lb, norm_gain):
    bsz, s, _ = q.shape

    def heads(t, d):
        return t.reshape(bsz, s, C_HEADS, d).astype(jnp.float32)

    qh = jax.nn.silu(heads(q, C_DK))
    vh = heads(inp, C_DV)
    lb = lb.reshape(C_HEADS, C_DK)
    log_lb = jnp.log(lb)

    def gates(fz):
        fz = heads(fz, C_DK)
        log_f = jnp.logaddexp(log_lb, jnp.log1p(-lb) + jax.nn.log_sigmoid(fz))
        k = (1.0 - lb) * jax.nn.sigmoid(-fz)
        return log_f, k

    lf_f, k_f = gates(f_fwd)
    lf_b, k_b = gates(f_bwd)
    o_f = gla_chunk_scan(qh, k_f, lf_f, vh)
    flip = lambda t: jnp.flip(t, axis=1)
    o_b = flip(gla_chunk_scan(flip(qh), flip(k_b), flip(lf_b), flip(vh)))
    o = o_f + o_b
    o = o * lax.rsqrt(jnp.mean(o * o, axis=-1, keepdims=True) + NORM_EPS)
    o = o * norm_gain.astype(jnp.float32).reshape(C_HEADS, C_DV)
    return o.reshape(bsz, s, C_WIDTH) * jax.nn.silu(gate.astype(jnp.float32))

def setup_inputs(seed: int = 0) -> dict:
    key = jax.random.key(seed)
    ks = jax.random.split(key, 12)
    f32 = jnp.float32

    def dense(k, shape, fan_in):
        return jax.random.normal(k, shape, f32) * (fan_in ** -0.5)

    return {
        "x": jax.random.normal(ks[0], (BATCH, SEQ, D_MODEL), f32),
        "pre_norm": 1.0 + 0.05 * jax.random.normal(ks[1], (DEPTH, D_MODEL), f32),
        "post_norm": 1.0 + 0.05 * jax.random.normal(ks[2], (DEPTH, D_MODEL), f32),
        "w_in": dense(ks[3], (DEPTH, D_MODEL, IN_COLS), D_MODEL),
        "sink_logits": 0.5 * jax.random.normal(ks[4], (DEPTH, B_Q_HEADS), f32),
        "hgrn_lower_bounds": 0.5 * jax.random.normal(ks[5], (DEPTH, C_HEADS * C_DK), f32),
        "hgrn_norm": 1.0 + 0.05 * jax.random.normal(ks[6], (DEPTH, C_WIDTH), f32),
        "w_branch_a": dense(ks[7], (DEPTH, A_WIDTH, D_MODEL), A_WIDTH),
        "w_branch_b": dense(ks[8], (DEPTH, B_WIDTH, D_MODEL), B_WIDTH),
        "w_branch_c": dense(ks[9], (DEPTH, C_WIDTH, D_MODEL), C_WIDTH),
        "w_out": dense(ks[10], (DEPTH, D_MODEL, D_MODEL), D_MODEL),
    }

def reference(x, pre_norm, post_norm, w_in, sink_logits, hgrn_lower_bounds, hgrn_norm,
              w_branch_a, w_branch_b, w_branch_c, w_out):
    bsz, s, _ = x.shape
    cos, sin = rope_tables(s)
    lb_all = jnp.cumsum(jax.nn.softmax(hgrn_lower_bounds.astype(jnp.float32), axis=0), axis=0)
    lb_all = lb_all - lb_all[0:1]
    split_points = [int(p) for p in np.cumsum(SPLIT_SIZES)[:-1]]
    for layer in range(DEPTH):
        xn = rms_norm(x, pre_norm[layer])
        proj = xn @ w_in[layer]
        (a_qkv, a_gate, b_q, b_k, b_v, b_gate,
         c_q, c_ff, c_fb, c_i, c_gate, merge) = jnp.split(proj, split_points, axis=-1)

        a_qkv = a_qkv.reshape(bsz, s, 3, A_HEADS, HEAD_DIM)
        qa = apply_partial_rope(a_qkv[:, :, 0], cos, sin)
        ka = apply_partial_rope(a_qkv[:, :, 1], cos, sin)
        ya = dilated_attention(qa, ka, a_qkv[:, :, 2]) * jax.nn.silu(a_gate.astype(jnp.float32))

        qb = apply_partial_rope(b_q.reshape(bsz, s, B_Q_HEADS, HEAD_DIM), cos, sin)
        kb = apply_partial_rope(b_k.reshape(bsz, s, B_KV_HEADS, HEAD_DIM), cos, sin)
        vb = b_v.reshape(bsz, s, B_KV_HEADS, HEAD_DIM)
        ob, _ = banded_window_attention(qb, kb, vb, B_HALF_WINDOW, sink=sink_logits[layer])
        yb = ob.reshape(bsz, s, B_WIDTH) * jax.nn.silu(b_gate.astype(jnp.float32))

        yc = hgrn2_bidirectional(c_q, c_ff, c_fb, c_i, c_gate, lb_all[layer], hgrn_norm[layer])

        g = jax.nn.sigmoid(merge.astype(jnp.float32)).reshape(bsz, s, N_BRANCHES, D_MODEL)
        dt = x.dtype
        y = (g[:, :, 0] * (ya.astype(dt) @ w_branch_a[layer])
             + g[:, :, 1] * (yb.astype(dt) @ w_branch_b[layer])
             + g[:, :, 2] * (yc.astype(dt) @ w_branch_c[layer]))
        out = y.astype(dt) @ w_out[layer]
        x = x + rms_norm(out, post_norm[layer])
    return x


_drawn_inputs = setup_inputs


def setup_inputs(seed=0):
    import zlib

    import numpy as np

    out = dict(_drawn_inputs(seed))
    spreads = {}
    factors = {'sink_logits': 8.0}
    for name, (base, spread) in spreads.items():
        noise = np.random.default_rng([zlib.crc32(name.encode()), seed]).standard_normal(out[name].shape)
        drawn = base * np.exp(spread * noise) if base else spread * noise
        out[name] = __import__('jax').numpy.asarray(drawn.astype(out[name].dtype))
    for name, factor in factors.items():
        out[name] = (out[name] * factor).astype(out[name].dtype)
    return out
```

```python
from contextlib import ExitStack

import numpy as np

import concourse.bass as bass
from concourse import mybir

ALU = mybir.AluOpType
ACT = mybir.ActivationFunctionType
AX = mybir.AxisListType
F32 = mybir.dt.float32
F32R = mybir.dt.float32r
BF16 = mybir.dt.bfloat16
U8 = mybir.dt.uint8

P = 128
D = 2048
T = 256
MT = T // P
DEPTH = 2
KT = D // P
CW = 512
QK = 4
TILE = QK * CW
EPS = 1e-6
HD = 128
ROT = HD // 4
HALF = ROT // 2
THETA = 500000.0
SCALE = float(HD) ** -0.5
NEG = -1e30
GROUPS = ((128, 1), (512, 4), (2048, 16))
NG = len(GROUPS)
SLOTS = D // 512
BQ = D // 256
BKV = BQ // 4
BWIN = 128
CH = D // 256
LEVELS = 8
TINY = 1e-18
LN_TINY = float(-np.log(TINY))

CHUNKS = [("gate_a", 0, KT)]
CHUNKS += [("rope_qa", g, KT) for g in range(NG)] + [("rope_ka", g, KT) for g in range(NG)]
CHUNKS += [("v_a", g, KT) for g in range(NG)]
CHUNKS += [("gate_b", 0, KT), ("gate_b", 1, KT), ("rope_qb", 0, KT), ("rope_qb", 1, KT), ("rope_kv", 0, KT)]
for _g in range(2):
    CHUNKS += [(k, _g, KT) for k in ("c_q", "c_zf", "c_zb", "c_v", "gate_c")]
for _b, _k in (("a", SLOTS), ("b", BQ), ("c", CH)):
    for _j in range(4):
        CHUNKS += [("merge_" + _b, _j, KT), ("z_" + _b, _j, _k)]
CHUNKS += [("out", j, KT) for j in range(4)]

STEP_OF = []
STEPS = []
for _c, (_kind, _i, _k) in enumerate(CHUNKS):
    STEP_OF.append(len(STEPS))
    STEPS += [(_c, q) for q in range(_k // QK)]
NSTEPS = len(STEPS)
ENDS = {}
for _c, (_kind, _i, _k) in enumerate(CHUNKS):
    ENDS[STEP_OF[_c] + _k // QK - 1] = _c


def end_of(kind, i):
    c = [n for n, x in enumerate(CHUNKS) if x[:2] == (kind, i)][0]
    return STEP_OF[c] + CHUNKS[c][2] // QK - 1


TURNED = [c for c, x in enumerate(CHUNKS) if x[0].startswith("rope") or x[0] in ("c_q", "c_zf", "c_zb")]
ROPED = [c for c in TURNED if CHUNKS[c][0].startswith("rope")]
MERGES = [c for c, x in enumerate(CHUNKS) if x[0].startswith("merge")]

A_UNITS = SLOTS * MT
B_UNITS = BKV * MT
UNITS = [end_of("v_a", NG - 1) + 2 + 2 * u for u in range(A_UNITS)]
UNITS += [end_of("rope_kv", 0) + 3 + 2 * u for u in range(B_UNITS)]
TURN_A = UNITS[A_UNITS - 1] + 5
TURN_B = [UNITS[-1] + 6, UNITS[-1] + 8]
REC = [TURN_B[1] + 2 + 15 * u for u in range(4)]
Z_A_END = end_of("z_a", 3)
TURN_C = [Z_A_END + 3, Z_A_END + 5, Z_A_END + 7, REC[3] + 17]
SP_EXTRA = REC[3] + 20
assert SP_EXTRA < end_of("merge_c", 3) and REC[3] + 20 < end_of("z_c", 0)

SILUS = [c for c, x in enumerate(CHUNKS) if x[0].startswith("gate") or x[0] == "c_q"]
SPLIT = 1280
PARAMS = KT + CH + BQ + DEPTH * CH + 1


def build(nc, W, X, CONST, MASKS, LMASKS, PAR, POST, OUT):
    out_v = OUT.rearrange("b (m p) d -> p (b m) d", p=P)
    x_v = X.rearrange("b (m p) d -> p (b m) d", p=P)
    with ExitStack() as ctx:
        def sb(name, shape, dt=F32):
            return ctx.enter_context(nc.sbuf_tensor(name, shape, dt))

        def sem(name):
            return ctx.enter_context(nc.semaphore(name))

        K1 = 1024
        place = (nc.sbuf_base + 31) // 32 * 32
        sb("arena_fence", [P, 76 * K1 // 4 + 8])
        arena = nc.alloc_sbuf_tensor_at("arena", [P, 76 * K1 // 4], F32, offset=place)

        raw = sb("raw", [P, 2, TILE])
        w_hi = sb("w_hi", [P, 2, TILE], F32R)
        w_lo = sb("w_lo", [P, 2, TILE], F32R)
        xT_hi = sb("xT_hi", [P, KT, T], F32R)
        xT_lo = sb("xT_lo", [P, KT, T], F32R)
        aT_hi = sb("aT_hi", [P, 4, T], F32R)
        aT_lo = sb("aT_lo", [P, 4, T], F32R)
        bT_hi = sb("bT_hi", [P, BQ, T], F32R)
        bT_lo = sb("bT_lo", [P, BQ, T], F32R)
        stage = sb("stage", [P, MT, CW])
        wide = sb("wide", [P, 1028 + 1024])
        scores = wide[:, 0:1028]
        probsT = wide[:, 1028:2052]
        ropes = sb("ropes", [P, 2, MT * 4 * ROT])
        const = sb("const", [P, P + MT * ROT * 2])
        masks = sb("masks", [P, MT, (NG + 1) * T], BF16)
        lmasks = sb("lmasks", [P, LEVELS - 1, P], U8)
        par = sb("par", [P, PARAMS])
        lbs = sb("lbs", [P, 8, CH])
        small = sb("small", [P, 64])
        small2 = sb("small2", [P, 64])
        half_neg = sb("half_neg", [P, 1])
        def piece(at, shape, dt=F32):
            n = int(np.prod(shape))
            v = arena[:, at * K1 // 4: at * K1 // 4 + n]
            if len(shape) == 2:
                return v.rearrange("p (a b) -> p a b", b=shape[1])
            if len(shape) == 3:
                return v.rearrange("p (a b c) -> p a b c", b=shape[1], c=shape[2])
            return v

        qaT = piece(0, [NG * SLOTS, T])
        kaT = piece(12, [NG * SLOTS, T])
        va = piece(24, [NG, MT, CW])
        gate_a = piece(36, [MT, CW])
        qbT = piece(40, [BQ, T])
        kbT = piece(48, [BKV, T])
        vb = piece(50, [MT, BKV * HD])
        gate_b = piece(52, [2, MT, CW])
        cq = [piece(20 * g, [4, T]) for g in range(2)]
        cz = [[piece(20 * g + 4, [4, T]), piece(20 * g + 8, [4, T])] for g in range(2)]
        cv = [piece(20 * g + 12, [MT, CW]) for g in range(2)]
        gate_c = [piece(20 * g + 16, [MT, CW]) for g in range(2)]
        PI = piece(40, [2, 512])
        RX = piece(44, [2, 512])
        EQ = piece(48, [4, 512])
        S_diag = piece(56, [4, P])
        S_off = piece(58, [4, P])
        y = piece(60, [MT, D])
        x_sb = piece(40, [MT, D])
        ident = const[:, 0:P]
        cosT = const[:, P:P + MT * ROT].rearrange("p (m r) -> p m r", m=MT)
        sinT = const[:, P + MT * ROT:P + 2 * MT * ROT].rearrange("p (m r) -> p m r", m=MT)
        pre_gain = par[:, 0:KT]
        hg_gain = par[:, KT:KT + CH]
        sink = par[:, KT + CH:KT + CH + BQ]
        lb_raw = par[:, KT + CH + BQ:KT + CH + BQ + DEPTH * CH].rearrange("p (l h) -> p l h", l=DEPTH)
        lb_sel = par[:, PARAMS - 1:PARAMS]
        lb, one_lb, lb_tiny = lbs[:, 0], lbs[:, 1], lbs[:, 2]
        sumsq = small[:, 0:2]
        rstd = small[:, 2:4]
        out_sq = small[:, 4:12]
        rec_sq = small[:, 12:16]
        rec_rstd = small[:, 16:20]
        smax = small2[:, 0:8].rearrange("p (b i) -> p b i", b=2)
        nmax = small2[:, 8:16].rearrange("p (b i) -> p b i", b=2)
        dens = small2[:, 16:24].rearrange("p (b i) -> p b i", b=2)
        rden = small2[:, 24:32].rearrange("p (b i) -> p b i", b=2)
        var = small2[:, 32:36]
        post_gain = wide[:, 0:D]

        yT_hi = nc.alloc_sbuf_tensor_at("yT_hi", [P, KT, T], F32R, offset=place + 8 * K1)
        yT_lo = nc.alloc_sbuf_tensor_at("yT_lo", [P, KT, T], F32R, offset=place + 24 * K1)
        cT_hi = nc.alloc_sbuf_tensor_at("cT_hi", [P, 4, T], F32R, offset=place)
        cT_lo = nc.alloc_sbuf_tensor_at("cT_lo", [P, 4, T], F32R, offset=place + 4 * K1)

        acc = [ctx.enter_context(nc.psum_tensor(f"acc{i}", [P, MT * CW], F32)) for i in range(2)]
        side = [ctx.enter_context(nc.psum_tensor(f"side{i}", [P, MT * CW], F32)) for i in range(2)]
        accv = [a[:, :].rearrange("p (m c) -> p m c", m=MT) for a in acc]

        x_stored = sem("x_stored")
        loaded = sem("loaded")
        w_landed = [sem("w_landed0"), sem("w_landed1")]
        par_landed = sem("par_landed")
        x_landed = sem("x_landed")
        hi_ready = sem("hi_ready")
        lo_dve = sem("lo_dve")
        lo_pool = sem("lo_pool")
        pe_step = sem("pe_step")
        acc_free = [sem("acc_free0"), sem("acc_free1")]
        dve_chain = sem("dve_chain")
        pool_chain = sem("pool_chain")
        act_chain = sem("act_chain")
        x_squared = sem("x_squared")
        x_rstd = sem("x_rstd")
        x_scaled = sem("x_scaled")
        x_turned = sem("x_turned")
        xT_hi_ready = sem("xT_hi_ready")
        xT_ready = sem("xT_ready")
        staged = sem("staged")
        roped = sem("roped")
        turned = sem("turned")
        tanhed = sem("tanhed")
        scored = sem("scored")
        masked = sem("masked")
        probs = sem("probs")
        probs_turned = sem("probs_turned")
        probs_copied = sem("probs_copied")
        attended = sem("attended")
        normed = sem("normed")
        branch_turned = sem("branch_turned")
        branch_hi = sem("branch_hi")
        branch_lo = sem("branch_lo")
        lb_ready = sem("lb_ready")
        rec_prep = sem("rec_prep")
        rec_exp = sem("rec_exp")
        mixed = sem("mixed")
        grams = sem("grams")
        decays = sem("decays")
        scanned = sem("scanned")
        kept = sem("kept")
        rec_out = sem("rec_out")
        rec_squared = sem("rec_squared")
        rec_rstd_ready = sem("rec_rstd_ready")
        rec_y = sem("rec_y")
        gated = sem("gated")
        summed = sem("summed")
        out_squared = sem("out_squared")
        out_summed = sem("out_summed")
        out_rstd = sem("out_rstd")
        x_new = sem("x_new")
        per_layer = [*w_landed, par_landed, x_landed, hi_ready, lo_dve, lo_pool, pe_step, *acc_free,
                     dve_chain, pool_chain, act_chain, x_squared, x_rstd, x_scaled, x_turned,
                     xT_hi_ready, xT_ready, staged, roped, turned, tanhed, scored, masked, probs,
                     probs_turned, probs_copied, attended, normed, branch_turned, branch_hi,
                     branch_lo, lb_ready, rec_prep, rec_exp, mixed, grams, decays, scanned, kept,
                     rec_out, rec_squared, rec_rstd_ready, rec_y, gated, summed, out_squared,
                     out_summed, out_rstd, x_new]

        turns = [(TURN_A, gate_a, 0, 4, aT_hi[:, :, :], aT_lo[:, :, :], None, side[0][:, :])]
        for r in range(2):
            turns.append((TURN_B[r], gate_b[:, r], 0, 4, bT_hi[:, 4 * r:4 * r + 4], bT_lo[:, 4 * r:4 * r + 4],
                          None, side[0][:, :]))
        for u in range(4):
            g, j = u // 2, 2 * (u % 2)
            hi, lo = (aT_hi, aT_lo) if g == 0 else (cT_hi, cT_lo)
            turns.append((TURN_C[u], gate_c[g], j, 2, hi[:, j:j + 2, :], lo[:, j:j + 2, :],
                          hg_gain[:, 4 * g + j:4 * g + j + 2], side[1][:, 512:1024]))
        for j in range(4):
            turns.append((end_of("z_c", j) + 2, y[:, :, j * CW:(j + 1) * CW], 0, 4, yT_hi[:, 4 * j:4 * j + 4, :],
                          yT_lo[:, 4 * j:4 * j + 4, :], None, side[j % 2][:, :]))
        TURN_AT = {t[0]: n for n, t in enumerate(turns)}

        def lhs(c, k):
            kind = CHUNKS[c][0]
            if kind == "out":
                return yT_hi[:, k, :], yT_lo[:, k, :]
            if kind == "z_a" or (kind == "z_c" and k < 4):
                return aT_hi[:, k, :], aT_lo[:, k, :]
            if kind == "z_b":
                return bT_hi[:, k, :], bT_lo[:, k, :]
            if kind == "z_c":
                return cT_hi[:, k - 4, :], cT_lo[:, k - 4, :]
            return xT_hi[:, k, :], xT_lo[:, k, :]

        def halves(v, level):
            w = v.rearrange("p (n two l) -> p n two l", two=2, l=1 << level)
            return w[:, :, 0, :], w[:, :, 1, :]

        def unit(u):
            if u < A_UNITS:
                h, m = divmod(u, MT)
                q = [qaT[:, g * SLOTS + h, m * P:(m + 1) * P] for g in range(NG)]
                k = [kaT[:, g * SLOTS + h, :] for g in range(NG)]
                return q, k, m
            kv, m = divmod(u - A_UNITS, MT)
            q = [qbT[:, 4 * kv + i, m * P:(m + 1) * P] for i in range(4)]
            return q, [kbT[:, kv, :]] * 4, m

        def rec_views(u):
            g, j = u // 2, 2 * (u % 2)
            flat = lambda v: v[:, j:j + 2, :].rearrange("p h t -> p (h t)")
            return flat(cq[g]), [flat(z) for z in cz[g]], cv[g], gate_c[g], 4 * g + j, j

        with nc.Block() as block:
            @block.sync
            def _(sp):
                sp.dma_start(x_sb, x_v).then_inc(loaded, 16)
                sp.dma_start(const[:, :], CONST).then_inc(loaded, 16)
                sp.dma_start(arena[:, 0:MT * (NG + 1) * T], MASKS).then_inc(loaded, 16)
                sp.dma_start(wide[:, 0:(LEVELS - 1) * P], LMASKS).then_inc(loaded, 16)
                sp.wait_ge(loaded, 64)
                sp.dma_start(out_v, x_sb).then_inc(x_stored, 16)

            @block.vector
            def _(dve):
                dve.memset(half_neg[:, :], -0.5)
                dve.wait_ge(loaded, 64)
                dve.tensor_copy(masks[:, :, :].rearrange("p m c -> p (m c)"), arena[:, 0:MT * (NG + 1) * T])
                dve.tensor_copy(lmasks[:, :, :].rearrange("p l c -> p (l c)"), wide[:, 0:(LEVELS - 1) * P])

        def evacuated(eng, c):
            eng.wait_ge(acc_free[c % 2], c // 2 + 1)

        def layer_body(layer, block):
            @block.sync
            def _(sp):
                for s in range(NSTEPS):
                    if s >= 2:
                        sp.wait_ge(lo_dve, s - 1)
                        sp.wait_ge(lo_pool, s - 1)
                    sp.dma_start(raw[:, s % 2, :], W[layer, s]).then_inc(w_landed[s % 2], 16)
                    if s == SP_EXTRA:
                        sp.wait_ge(x_stored, 16 * (layer + 1))
                        sp.wait_ge(branch_turned, 7)
                        sp.dma_start(x_sb, out_v).then_inc(x_landed, 16)
                        sp.dma_start(post_gain, POST[layer].partition_broadcast(P)).then_inc(x_landed, 16)
                sp.wait_ge(x_landed, 32)
                sp.wait_ge(x_new, 2)
                sp.dma_start(out_v, x_sb).then_inc(x_stored, 16)

            @block.gpsimd
            def _(pool):
                count = [0]

                def link(ins):
                    count[0] += 1
                    ins.then_inc(pool_chain, 1)
                    pool.wait_ge(pool_chain, count[0])

                def lo(s):
                    pool.wait_ge(hi_ready, s + 1)
                    if s >= 2:
                        pool.wait_ge(pe_step, s - 1)
                    pool.tensor_tensor(w_lo[:, s % 2, SPLIT:TILE], raw[:, s % 2, SPLIT:TILE],
                                       w_hi[:, s % 2, SPLIT:TILE].bitcast(F32), ALU.subtract).then_inc(lo_pool, 1)

                def power(dst, src, mean, done):
                    n = src.shape[1]
                    link(pool.tensor_scalar(dst, src, mean, EPS, ALU.mult, ALU.add))
                    pool.tensor_tensor(dst, dst, half_neg[:, :].broadcast_to([P, n]), ALU.pow).then_inc(done, 1)

                pool.wait_ge(x_squared, 2)
                power(rstd, sumsq, 1.0 / D, x_rstd)
                lo(0)
                for s in range(NSTEPS + 3):
                    if s + 1 < NSTEPS:
                        lo(s + 1)
                    for u in range(4):
                        l = s - REC[u] - 6
                        if 0 <= l < LEVELS - 1:
                            pool.wait_ge(decays, LEVELS * u + l + 1)
                            pf_lo, pf_up = halves(PI[:, 0], l)
                            rx_lo, _ = halves(RX[:, 0], l)
                            pb_lo, pb_up = halves(PI[:, 1], l)
                            _, rb_up = halves(RX[:, 1], l)
                            n, L = 512 >> (l + 1), 1 << l
                            last = lambda v: v[:, :, L - 1:L].broadcast_to([P, n, L])
                            head = lambda v: v[:, :, 0:1].broadcast_to([P, n, L])
                            pool.tensor_tensor(rx_lo, rx_lo, last(pf_up), ALU.add)
                            link(pool.tensor_tensor(rb_up, rb_up, head(pb_lo), ALU.add))
                            pool.tensor_tensor(pf_up, pf_up, last(pf_lo), ALU.add)
                            link(pool.tensor_tensor(pb_lo, pb_lo, head(pb_up), ALU.add))
                            pool.nop().then_inc(scanned, 1)
                        if s == REC[u] + 15:
                            pool.wait_ge(rec_squared, u + 1)
                            power(rec_rstd, rec_sq, 1.0 / HD, rec_rstd_ready)
                    c = ENDS.get(s - 1)
                    if c is not None and CHUNKS[c][0] in ("z_b", "z_c"):
                        n = [x for x in range(c + 1) if CHUNKS[x][0] in ("z_b", "z_c")]
                        j = CHUNKS[c][1]
                        pool.wait_ge(gated, len(n) + 4)
                        part = y[:, :, j * CW:(j + 1) * CW]
                        pool.tensor_tensor(part, part, stage[:, :, :], ALU.add).then_inc(summed, 1)
                pool.wait_ge(out_summed, 1)
                power(rstd, sumsq, 1.0 / D, out_rstd)

            @block.scalar
            def _(act):
                act.dma_start(par[:, :], PAR[layer]).then_inc(par_landed, 16)
                count = [0]

                def hi(s):
                    act.wait_ge(w_landed[s % 2], 16 * (s // 2 + 1))
                    if s >= 2:
                        act.wait_ge(pe_step, s - 1)
                    act.activation(w_hi[:, s % 2, :], raw[:, s % 2, :], ACT.Copy).then_inc(hi_ready, 1)

                for m in range(MT):
                    act.activation(y[:, m, :], x_sb[:, m, :], ACT.Square,
                                   accum_out=sumsq[:, m:m + 1]).then_inc(x_squared, 1)
                hi(0)
                act.wait_ge(lb_ready, 1)
                act.activation(lbs[:, 4:4 + DEPTH, :], lbs[:, 4:4 + DEPTH, :], ACT.Exp).then_inc(lb_ready, 1)
                act.wait_ge(par_landed, 16)
                for b in range(KT // 2):
                    act.wait_ge(x_turned, b + 1)
                    src = (acc[0], acc[1], side[0], side[1])[b // 2][:, (b % 2) * 512:(b % 2) * 512 + 512]
                    for i in range(2):
                        ins = act.activation(xT_hi[:, 2 * b + i, :], src[:, i * T:(i + 1) * T], ACT.Copy,
                                             scale=pre_gain[:, 2 * b + i:2 * b + i + 1])
                    ins.then_inc(xT_hi_ready, 1)

                for s in range(NSTEPS + 3):
                    if s + 1 < NSTEPS:
                        hi(s + 1)
                    c = ENDS.get(s - 1)
                    if c is not None:
                        kind, i, _ = CHUNKS[c]
                        act.wait_ge(pe_step, s)
                        if c in TURNED:
                            n = TURNED.index(c)
                            if n:
                                act.wait_ge(turned, n)
                            if kind == "rope_kv":
                                act.activation(vb, accv[c % 2][:, :, T:2 * T], ACT.Copy)
                                act.activation(stage[:, :, 0:T], accv[c % 2][:, :, 0:T], ACT.Copy).then_inc(staged, 1)
                            else:
                                act.activation(stage[:, :, :], accv[c % 2], ACT.Copy).then_inc(staged, 1)
                        elif kind in ("v_a", "c_v"):
                            if kind == "c_v":
                                act.wait_ge(branch_turned, 1)
                            act.activation(va[:, i] if kind == "v_a" else cv[i], accv[c % 2],
                                           ACT.Copy).then_inc(acc_free[c % 2], 1)
                        elif kind.startswith("gate"):
                            dst = {"gate_a": lambda: gate_a, "gate_b": lambda: gate_b[:, i],
                                   "gate_c": lambda: gate_c[i]}[kind]()
                            if kind == "gate_b" and i == 0:
                                act.wait_ge(x_stored, 16 * (layer + 1))
                            if kind == "gate_c":
                                act.wait_ge(branch_turned, 1)
                            act.activation(dst, accv[c % 2], ACT.Tanh, scale=0.5).then_inc(tanhed, 1)
                        elif kind.startswith("merge"):
                            n = MERGES.index(c)
                            if n == 0:
                                act.wait_ge(turned, len(TURNED))
                            elif n <= 4:
                                act.wait_ge(gated, n)
                            else:
                                act.wait_ge(summed, n - 4)
                            act.activation(stage[:, :, :], accv[c % 2], ACT.Tanh,
                                           scale=0.5).then_inc(acc_free[c % 2], 1)
                        elif kind == "out":
                            act.wait_ge(summed, 8)
                            if i:
                                act.wait_ge(out_squared, 2 * i)
                            for m in range(MT):
                                ins = act.activation(stage[:, m, :], accv[c % 2][:, m, :], ACT.Square,
                                                     accum_out=out_sq[:, 4 * m + i:4 * m + i + 1])
                                ins.then_inc(out_squared, 1)
                    c = ENDS.get(s - 2)
                    if c is not None and CHUNKS[c][0] in ("c_q", "c_zf", "c_zb"):
                        kind, i, _ = CHUNKS[c]
                        act.wait_ge(turned, TURNED.index(c) + 1)
                        act.wait_ge(branch_turned, 1)
                        src = acc[c % 2][:, :].rearrange("p (h t) -> p h t", h=4)
                        if kind == "c_q":
                            act.activation(cq[i], src, ACT.Tanh, scale=0.5).then_inc(tanhed, 1)
                        else:
                            act.activation(cz[i][kind == "c_zb"], src, ACT.Copy).then_inc(acc_free[c % 2], 1)
                    c = ENDS.get(s - 3)
                    if c is not None and c in ROPED:
                        kind, i, _ = CHUNKS[c]
                        act.wait_ge(turned, TURNED.index(c) + 1)
                        dst = {"rope_qa": qaT, "rope_ka": kaT, "rope_qb": qbT, "rope_kv": kbT}[kind]
                        if kind != "rope_kv":
                            dst = dst[:, 4 * i:4 * i + 4]
                        nh = dst.shape[1]
                        act.activation(dst, acc[c % 2][:, 0:nh * T].rearrange("p (h t) -> p h t", h=nh),
                                       ACT.Copy).then_inc(acc_free[c % 2], 1)
                    for u, s0 in enumerate(UNITS):
                        if s == s0 + 2:
                            act.wait_ge(masked, u + 1)
                            b = u % 2
                            if u < A_UNITS:
                                act.activation(scores[:, 0:NG * T], scores[:, 0:NG * T], ACT.Exp, bias=nmax[:, b, 0:1],
                                               scale=SCALE, accum_out=dens[:, b, 0:1]).then_inc(probs, 1)
                            else:
                                for i in range(4):
                                    v = scores[:, 257 * i:257 * i + 257]
                                    ins = act.activation(v, v, ACT.Exp, bias=nmax[:, b, i:i + 1], scale=SCALE,
                                                         accum_out=dens[:, b, i:i + 1])
                                    if i == 3:
                                        ins.then_inc(probs, 1)
                        if s == s0 + 3:
                            act.wait_ge(probs_turned, u + 1)
                            if u:
                                act.wait_ge(attended, u)
                            n = NG * T if u < A_UNITS else 4 * T
                            act.activation(probsT[:, 0:n], side[1][:, 0:n], ACT.Copy).then_inc(probs_copied, 1)
                    if s - 1 in TURN_AT:
                        n = TURN_AT[s - 1]
                        _, _, _, blocks, dst, _, gain, ps = turns[n]
                        act.wait_ge(branch_turned, n + 1)
                        src = ps.rearrange("p (i t) -> p i t", t=T)
                        if gain is None:
                            act.activation(dst, src, ACT.Copy, scale=0.5).then_inc(branch_hi, 1)
                        else:
                            for i in range(blocks):
                                ins = act.activation(dst[:, i], src[:, i], ACT.Copy, scale=gain[:, i:i + 1])
                            ins.then_inc(branch_hi, 1)
                    for u in range(4):
                        d = s - REC[u]
                        if d == 1:
                            act.wait_ge(rec_prep, 2 * u + 1)
                            act.activation(EQ, EQ, ACT.Exp).then_inc(rec_exp, 1)
                        if d == 4:
                            act.wait_ge(rec_prep, 2 * u + 2)
                            act.activation(EQ[:, 0:2], EQ[:, 0:2], ACT.Ln).then_inc(rec_exp, 1)
                        l = d - 6
                        if 0 <= l < LEVELS:
                            act.wait_ge(mixed, (LEVELS + 1) * u + l + 1)
                            if l:
                                act.wait_ge(scanned, (LEVELS - 1) * u + l)
                            ef_lo, ef_up = halves(EQ[:, 0], l)
                            eb_lo, eb_up = halves(EQ[:, 1], l)
                            act.activation(ef_up, halves(PI[:, 0], l)[1], ACT.Exp)
                            act.activation(ef_lo, halves(RX[:, 0], l)[0], ACT.Exp)
                            act.activation(eb_lo, halves(PI[:, 1], l)[0], ACT.Exp)
                            act.activation(eb_up, halves(RX[:, 1], l)[1], ACT.Exp).then_inc(decays, 1)
                        if d == 15:
                            act.wait_ge(rec_out, u + 1)
                            for i in range(4):
                                ins = act.activation(wide[:, i * P:(i + 1) * P], side[1][:, i * P:(i + 1) * P], ACT.Square,
                                                     scale=0.5, accum_out=rec_sq[:, i:i + 1])
                            ins.then_inc(rec_squared, 1)

            @block.vector
            def _(dve):
                count = [0]

                def link(ins):
                    count[0] += 1
                    ins.then_inc(dve_chain, 1)
                    dve.wait_ge(dve_chain, count[0])

                def lo(s):
                    dve.wait_ge(hi_ready, s + 1)
                    if s >= 2:
                        dve.wait_ge(pe_step, s - 1)
                    dve.tensor_tensor(w_lo[:, s % 2, 0:SPLIT], raw[:, s % 2, 0:SPLIT],
                                      w_hi[:, s % 2, 0:SPLIT].bitcast(F32), ALU.subtract).then_inc(lo_dve, 1)

                dve.wait_ge(x_rstd, 1)
                for m in range(MT):
                    dve.tensor_scalar(y[:, m, :], x_sb[:, m, :], rstd[:, m:m + 1], None, ALU.mult).then_inc(x_scaled, 1)
                lo(0)
                dve.wait_ge(par_landed, 16)
                link(dve.tensor_tensor(lbs[:, 3], lb_raw[:, 0], lb_raw[:, 1], ALU.max))
                dve.tensor_tensor(lbs[:, 4], lb_raw[:, 0], lbs[:, 3], ALU.subtract)
                dve.tensor_tensor(lbs[:, 5], lb_raw[:, 1], lbs[:, 3], ALU.subtract).then_inc(lb_ready, 1)
                for b in range(KT // 2):
                    dve.wait_ge(xT_hi_ready, b + 1)
                    src = (acc[0], acc[1], side[0], side[1])[b // 2][:, (b % 2) * 512:(b % 2) * 512 + 512]
                    for i in range(2):
                        k = 2 * b + i
                        ins = dve.scalar_tensor_tensor(out=xT_lo[:, k, :], in0=src[:, i * T:(i + 1) * T],
                                                       scalar=pre_gain[:, k:k + 1], in1=xT_hi[:, k, :].bitcast(F32),
                                                       op0=ALU.mult, op1=ALU.subtract)
                    ins.then_inc(xT_ready, 1)
                dve.wait_ge(lb_ready, 2)
                link(dve.tensor_tensor(lbs[:, 6], lbs[:, 4], lbs[:, 5], ALU.add))
                link(dve.reciprocal(lbs[:, 6], lbs[:, 6]))
                link(dve.tensor_tensor(lbs[:, 6], lbs[:, 6], lbs[:, 5], ALU.mult))
                link(dve.tensor_scalar(lb, lbs[:, 6], lb_sel, None, ALU.mult))
                dve.tensor_scalar(one_lb, lb, -1.0, 1.0, ALU.mult, ALU.add)
                dve.tensor_scalar(lb_tiny, lb, TINY, None, ALU.is_lt)
                link(dve.tensor_scalar(hg_gain, hg_gain, 0.25, None, ALU.mult))
                link(dve.tensor_scalar(sink, sink, 1.0 / SCALE, None, ALU.mult))

                def rope(c, n):
                    dve.wait_ge(staged, TURNED.index(c) + 1)
                    st = stage[:, :, 0:n * HD].rearrange("p m (h d) -> p m h d", d=HD)
                    ta = ropes[:, 0, 0:MT * n * ROT].rearrange("p (m h r) -> p m h r", m=MT, h=n)
                    tb = ropes[:, 1, 0:MT * n * ROT].rearrange("p (m h r) -> p m h r", m=MT, h=n)
                    wide_ = lambda v, w: v[:, :, None, :].broadcast_to([P, MT, n, w])
                    dve.tensor_tensor(ta, st[:, :, :, 0:ROT], wide_(cosT, ROT), ALU.mult)
                    dve.tensor_tensor(tb[:, :, :, 0:HALF], st[:, :, :, HALF:ROT], wide_(sinT[:, :, 0:HALF], HALF), ALU.mult)
                    link(dve.tensor_tensor(tb[:, :, :, HALF:ROT], st[:, :, :, 0:HALF], wide_(sinT[:, :, HALF:ROT], HALF),
                                           ALU.mult))
                    dve.tensor_tensor(st[:, :, :, 0:ROT], ta, tb, ALU.add).then_inc(roped, 1)

                for s in range(NSTEPS + 3):
                    if s + 1 < NSTEPS:
                        lo(s + 1)
                    for u in range(4):
                        d = s - REC[u]
                        q, z, _, gate, head, j = rec_views(u)
                        nine = (LEVELS + 1) * u
                        if d == 0:
                            if u == 0:
                                dve.wait_ge(branch_turned, 3)
                            else:
                                dve.wait_ge(grams, nine)
                            evacuated(dve, CHUNKS.index(("c_zb", u // 2, KT)))
                            for x in range(2):
                                dve.tensor_scalar(EQ[:, x], z[x], 0.0, None, ALU.min)
                                dve.tensor_scalar(EQ[:, 2 + x], z[x], -1.0, 0.0, ALU.mult, ALU.min)
                                ins = dve.tensor_scalar(PI[:, x], z[x], LN_TINY, 0.0, ALU.add, ALU.min)
                            ins.then_inc(rec_prep, 1)
                        if d == 2:
                            dve.wait_ge(rec_exp, 2 * u + 1)
                            link(dve.tensor_tensor(RX, EQ[:, 0:2], EQ[:, 2:4], ALU.add))
                            link(dve.reciprocal(RX, RX))
                            for x in range(2):
                                for h in range(2):
                                    cols = slice(h * T, (h + 1) * T)
                                    ins = dve.scalar_tensor_tensor(
                                        out=z[x][:, cols], in0=EQ[:, 2 + x, cols], scalar=one_lb[:, head + h:head + h + 1],
                                        in1=RX[:, x, cols], op0=ALU.mult, op1=ALU.mult)
                            link(ins)
                        if d == 3:
                            for x in range(2):
                                for h in range(2):
                                    cols = slice(h * T, (h + 1) * T)
                                    ins = dve.scalar_tensor_tensor(
                                        out=EQ[:, x, cols], in0=EQ[:, 2 + x, cols], scalar=lb[:, head + h:head + h + 1],
                                        in1=EQ[:, x, cols], op0=ALU.mult, op1=ALU.add)
                            link(ins)
                            link(dve.tensor_tensor(EQ[:, 0:2], EQ[:, 0:2], RX, ALU.mult))
                            dve.tensor_scalar(EQ[:, 0:2], EQ[:, 0:2], TINY, None, ALU.max).then_inc(rec_prep, 1)
                        if d == 5:
                            dve.wait_ge(rec_exp, 2 * u + 2)
                            for x in range(2):
                                for h in range(2):
                                    cols = slice(h * T, (h + 1) * T)
                                    dve.scalar_tensor_tensor(
                                        out=PI[:, x, cols], in0=PI[:, x, cols], scalar=lb_tiny[:, head + h:head + h + 1],
                                        in1=EQ[:, x, cols], op0=ALU.mult, op1=ALU.add)
                            dve.memset(RX, 0.0)
                            dve.tensor_tensor(EQ[:, 2], z[0], z[1], ALU.add).then_inc(mixed, 1)
                        l = d - 6
                        if 0 <= l < LEVELS:
                            dve.wait_ge(grams, nine + l + 1)
                            src = side[0][:, (nine + l) % 2 * 512:(nine + l) % 2 * 512 + 512].rearrange(
                                "p (b t) -> p b t", t=P)
                            if l == 0:
                                if u:
                                    dve.wait_ge(rec_out, u)
                                ins = dve.tensor_copy(S_diag, src)
                            else:
                                dve.wait_ge(kept, nine + l)
                                ins = dve.copy_predicated(S_diag, lmasks[:, l - 1:l, :].broadcast_to([P, 4, P]), src)
                            ins.then_inc(kept, 1)
                            dve.wait_ge(decays, LEVELS * u + l + 1)
                            (ef_lo, ef_up), (eb_lo, eb_up) = halves(EQ[:, 0], l), halves(EQ[:, 1], l)
                            (k_lo, k_up), (q_lo, q_up) = halves(EQ[:, 2], l), halves(EQ[:, 3], l)
                            dve.tensor_tensor(k_lo, halves(z[0], l)[0], ef_lo, ALU.mult)
                            dve.tensor_tensor(k_up, halves(z[1], l)[1], eb_up, ALU.mult)
                            dve.tensor_tensor(q_up, halves(q, l)[1], ef_up, ALU.mult)
                            dve.tensor_tensor(q_lo, halves(q, l)[0], eb_lo, ALU.mult).then_inc(mixed, 1)
                        if d == 14:
                            dve.wait_ge(grams, nine + LEVELS + 1)
                            dve.tensor_copy(S_off, side[0][:, (nine + LEVELS) % 2 * 512:(nine + LEVELS) % 2 * 512 + 512]
                                            .rearrange("p (b t) -> p b t", t=P)).then_inc(kept, 1)
                        if d == 16:
                            dve.wait_ge(rec_rstd_ready, u + 1)
                            evacuated(dve, CHUNKS.index(("gate_c", u // 2, KT)))
                            for h in range(2):
                                for m in range(MT):
                                    i = h * MT + m
                                    part = gate[:, m, (j + h) * HD:(j + h + 1) * HD]
                                    ins = dve.scalar_tensor_tensor(out=part, in0=side[1][:, i * P:(i + 1) * P],
                                                                   scalar=rec_rstd[:, i:i + 1], in1=part,
                                                                   op0=ALU.mult, op1=ALU.mult)
                            ins.then_inc(rec_y, 1)
                    for u, s0 in enumerate(UNITS):
                        b = u % 2
                        m = unit(u)[2]
                        nh = 1 if u < A_UNITS else 4
                        if s == s0 + 1:
                            dve.wait_ge(scored, u + 1)
                            if u:
                                dve.wait_ge(probs_turned, u)
                            if u < A_UNITS:
                                v = scores[:, 0:NG * T]
                                link(dve.tensor_tensor(v, side[0][:, 0:NG * T], masks[:, m, 0:NG * T], ALU.add))
                                link(dve.reduce_max(smax[:, b, 0:1], v, AX.X))
                            else:
                                v = scores.rearrange("p (i t) -> p i t", i=4)
                                kv = (u - A_UNITS) // MT
                                dve.tensor_copy(v[:, :, T], sink[:, 4 * kv:4 * kv + 4])
                                link(dve.tensor_tensor(v[:, :, 0:T], side[0][:, :].rearrange("p (i t) -> p i t", i=4),
                                                       masks[:, m:m + 1, NG * T:(NG + 1) * T].broadcast_to([P, 4, T]), ALU.add))
                                link(dve.reduce_max(smax[:, b, :], v, AX.X))
                            dve.tensor_scalar(nmax[:, b, 0:nh], smax[:, b, 0:nh], -SCALE, None, ALU.mult).then_inc(masked, 1)
                        if s == s0 + 3:
                            dve.wait_ge(probs, u + 1)
                            link(dve.reciprocal(rden[:, b, 0:nh], dens[:, b, 0:nh]))
                        if s == s0 + 4:
                            dve.wait_ge(attended, u + 1)
                            for i in range(nh):
                                if u < A_UNITS:
                                    if u == 0:
                                        evacuated(dve, 0)
                                    h = u // MT
                                    part = gate_a[:, m, h * HD:(h + 1) * HD]
                                else:
                                    part = gate_b[:, (u - A_UNITS) // MT, m, i * HD:(i + 1) * HD]
                                ins = dve.scalar_tensor_tensor(out=part, in0=side[1][:, i * P:(i + 1) * P],
                                                               scalar=rden[:, b, i:i + 1], in1=part,
                                                               op0=ALU.mult, op1=ALU.mult)
                            ins.then_inc(normed, 1)
                    if s - 1 in TURN_AT:
                        n = TURN_AT[s - 1]
                        _, _, _, blocks, hi_, lo_, gain, ps = turns[n]
                        dve.wait_ge(branch_hi, n + 1)
                        src = ps.rearrange("p (i t) -> p i t", t=T)
                        if gain is None:
                            dve.scalar_tensor_tensor(out=lo_, in0=src, scalar=0.5, in1=hi_.bitcast(F32), op0=ALU.mult,
                                                     op1=ALU.subtract).then_inc(branch_lo, 1)
                        else:
                            for i in range(blocks):
                                ins = dve.scalar_tensor_tensor(out=lo_[:, i], in0=src[:, i], scalar=gain[:, i:i + 1],
                                                               in1=hi_[:, i].bitcast(F32), op0=ALU.mult, op1=ALU.subtract)
                            ins.then_inc(branch_lo, 1)
                    c = ENDS.get(s - 1)
                    if c is not None and CHUNKS[c][0].startswith("z_"):
                        kind, j, _ = CHUNKS[c]
                        dve.wait_ge(pe_step, s)
                        evacuated(dve, c - 1)
                        dst = y[:, :, j * CW:(j + 1) * CW] if kind == "z_a" else stage[:, :, :]
                        if kind == "z_a" and j == 0:
                            dve.wait_ge(x_turned, KT // 2)
                        dve.scalar_tensor_tensor(out=dst, in0=stage[:, :, :], scalar=1.0, in1=accv[c % 2], op0=ALU.add,
                                                 op1=ALU.mult).then_inc(gated, 1)
                        dve.wait_ge(gated, (c - CHUNKS.index(("merge_a", 0, KT)) + 1) // 2)
                        dve.nop().then_inc(acc_free[c % 2], 1)
                    c = ENDS.get(s - 2)
                    if c is not None:
                        kind, i, _ = CHUNKS[c]
                        if kind.startswith("rope"):
                            rope(c, 2 if kind == "rope_kv" else 4)
                        if kind.startswith("gate"):
                            dve.wait_ge(tanhed, SILUS.index(c) + 1)
                            dst = {"gate_a": lambda: gate_a, "gate_b": lambda: gate_b[:, i],
                                   "gate_c": lambda: gate_c[i]}[kind]()
                            dve.scalar_tensor_tensor(out=dst, in0=dst, scalar=1.0, in1=accv[c % 2], op0=ALU.add,
                                                     op1=ALU.mult).then_inc(acc_free[c % 2], 1)
                        if kind == "out":
                            dve.wait_ge(out_squared, 2 * (i + 1))
                            dve.wait_ge(branch_turned, 8 + i)
                            if i == 0:
                                dve.wait_ge(x_landed, 32)
                            dve.tensor_tensor(y[:, :, i * CW:(i + 1) * CW], accv[c % 2],
                                              post_gain[:, None, i * CW:(i + 1) * CW].broadcast_to([P, MT, CW]),
                                              ALU.mult).then_inc(acc_free[c % 2], 1)
                    c = ENDS.get(s - 3)
                    if c is not None and CHUNKS[c][0] == "c_q":
                        dve.wait_ge(tanhed, SILUS.index(c) + 1)
                        dst = cq[CHUNKS[c][1]]
                        dve.scalar_tensor_tensor(out=dst, in0=dst, scalar=1.0,
                                                 in1=acc[c % 2][:, :].rearrange("p (h t) -> p h t", h=4),
                                                 op0=ALU.add, op1=ALU.mult).then_inc(acc_free[c % 2], 1)
                dve.tensor_reduce(sumsq, out_sq.rearrange("p (m j) -> p m j", m=MT), AX.X, ALU.add).then_inc(out_summed, 1)
                dve.wait_ge(out_rstd, 1)
                evacuated(dve, len(CHUNKS) - 1)
                evacuated(dve, len(CHUNKS) - 2)
                for m in range(MT):
                    dve.scalar_tensor_tensor(out=x_sb[:, m, :], in0=y[:, m, :], scalar=rstd[:, m:m + 1],
                                             in1=x_sb[:, m, :], op0=ALU.mult, op1=ALU.add).then_inc(x_new, 1)

            @block.tensor
            def _(pe):
                def mm(out, a, b, start=True, stop=True):
                    return pe.matmul(out, a, b, start=start, stop=stop)

                for b in range(KT // 2):
                    dst = (acc[0], acc[1], side[0], side[1])[b // 2][:, (b % 2) * 512:(b % 2) * 512 + 512]
                    for m in range(MT):
                        if b == 0:
                            pe.wait_ge(x_scaled, m + 1)
                        for i in range(2):
                            k = 2 * b + i
                            ins = pe.transpose(dst[:, i * T + m * P:i * T + (m + 1) * P], y[:, m, k * P:(k + 1) * P], ident)
                    ins.then_inc(x_turned, 1)

                def stream(s):
                    c, q = STEPS[s]
                    kind, i, k = CHUNKS[c]
                    slot = s % 2
                    if q == 0 and c >= 2:
                        pe.wait_ge(acc_free[c % 2], c // 2)
                    if c == 0:
                        pe.wait_ge(xT_ready, 2 * (q + 1))
                    if kind[:2] == "z_" and i == 0 and q == 0:
                        pe.wait_ge(branch_lo, {"z_a": 1, "z_b": 3, "z_c": 7}[kind])
                    if kind == "out" and i == 0:
                        pe.wait_ge(branch_lo, 8 + q)
                    pe.wait_ge(hi_ready, s + 1)
                    for t in range(QK):
                        w = w_hi[:, slot, t * CW:(t + 1) * CW]
                        for n, part in enumerate(lhs(c, QK * q + t)):
                            for m in range(MT):
                                mm(acc[c % 2][:, m * CW:(m + 1) * CW], part[:, m * P:(m + 1) * P], w,
                                   start=(q == 0 and t == 0 and n == 0), stop=False)
                    pe.wait_ge(lo_dve, s + 1)
                    pe.wait_ge(lo_pool, s + 1)
                    for t in range(QK):
                        w = w_lo[:, slot, t * CW:(t + 1) * CW]
                        part = lhs(c, QK * q + t)[0]
                        for m in range(MT):
                            ins = mm(acc[c % 2][:, m * CW:(m + 1) * CW], part[:, m * P:(m + 1) * P], w, start=False,
                                     stop=(q == k // QK - 1 and t == QK - 1))
                    ins.then_inc(pe_step, 1)

                def turn(c):
                    n = 2 if CHUNKS[c][0] == "rope_kv" else 4
                    if c in ROPED:
                        pe.wait_ge(roped, ROPED.index(c) + 1)
                    else:
                        pe.wait_ge(staged, TURNED.index(c) + 1)
                    for h in range(n):
                        for m in range(MT):
                            ins = pe.transpose(acc[c % 2][:, h * T + m * P:h * T + (m + 1) * P],
                                               stage[:, m, h * HD:(h + 1) * HD], ident)
                    ins.then_inc(turned, 1)

                for s in range(NSTEPS):
                    stream(s)
                    c = ENDS.get(s - 1)
                    if c is not None and c in TURNED and c not in ROPED:
                        turn(c)
                    c = ENDS.get(s - 2)
                    if c is not None and c in ROPED:
                        turn(c)
                    for u, s0 in enumerate(UNITS):
                        q, k, m = unit(u)
                        if s == s0:
                            if u == 0:
                                for g in range(2 * NG):
                                    evacuated(pe, 1 + g)
                            elif u == A_UNITS:
                                for g in range(3):
                                    evacuated(pe, CHUNKS.index(("rope_qb", 0, KT)) + g)
                                pe.wait_ge(branch_lo, 1)
                            if u:
                                pe.wait_ge(masked, u)
                            for i in range(len(q)):
                                ins = mm(side[0][:, i * T:(i + 1) * T], q[i], k[i])
                            ins.then_inc(scored, 1)
                        if s == s0 + 2:
                            pe.wait_ge(probs, u + 1)
                            if u:
                                pe.wait_ge(normed, u)
                            for i in range(len(q)):
                                for t in range(MT):
                                    at = (257 if u >= A_UNITS else T) * i + t * P
                                    ins = pe.transpose(side[1][:, (2 * i + t) * P:(2 * i + t + 1) * P], scores[:, at:at + P],
                                                       ident)
                            ins.then_inc(probs_turned, 1)
                        if s == s0 + 3:
                            pe.wait_ge(probs_copied, u + 1)
                            if u == 0:
                                for g in range(NG):
                                    evacuated(pe, 1 + 2 * NG + g)
                            for i in range(len(q)):
                                for t in range(MT):
                                    w = probsT[:, (2 * i + t) * P:(2 * i + t + 1) * P]
                                    if u < A_UNITS:
                                        h = u // MT
                                        ins = mm(side[1][:, 0:P], w, va[:, i, t, h * HD:(h + 1) * HD],
                                                 start=(i == 0 and t == 0), stop=(i == NG - 1 and t == MT - 1))
                                    else:
                                        kv = (u - A_UNITS) // MT
                                        ins = mm(side[1][:, i * P:(i + 1) * P], w, vb[:, t, kv * HD:(kv + 1) * HD],
                                                 start=(t == 0), stop=(t == MT - 1))
                            ins.then_inc(attended, 1)
                    for u in range(4):
                        d = s - REC[u]
                        q, _, v, _, _, j = rec_views(u)
                        nine = (LEVELS + 1) * u
                        if 5 <= d < 6 + LEVELS:
                            l = d - 6
                            n = nine + l + 1
                            pe.wait_ge(mixed, n + 1)
                            if n >= 2:
                                pe.wait_ge(kept, n - 1)
                            if n == 0:
                                pe.wait_ge(branch_lo, 3)
                            dst = side[0][:, n % 2 * 512:n % 2 * 512 + 512]
                            for b in range(4):
                                h, st = divmod(b, 2)
                                tt = 1 - st if l == LEVELS - 1 else st
                                qq = q if l < 0 else EQ[:, 3]
                                ins = mm(dst[:, b * P:(b + 1) * P], EQ[:, 2, h * T + st * P:h * T + (st + 1) * P],
                                         qq[:, h * T + tt * P:h * T + (tt + 1) * P])
                            ins.then_inc(grams, 1)
                        if d == 14:
                            pe.wait_ge(kept, nine + LEVELS + 1)
                            evacuated(pe, CHUNKS.index(("c_v", u // 2, KT)))
                            if u:
                                pe.wait_ge(rec_y, u)
                            for h in range(2):
                                for tt in range(MT):
                                    i = h * MT + tt
                                    o = side[1][:, i * P:(i + 1) * P]
                                    mm(o, S_diag[:, i], v[:, tt, (j + h) * HD:(j + h + 1) * HD], stop=False)
                                    ins = mm(o, S_off[:, h * MT + 1 - tt], v[:, 1 - tt, (j + h) * HD:(j + h + 1) * HD],
                                             start=False)
                            ins.then_inc(rec_out, 1)
                    if s in TURN_AT:
                        n = TURN_AT[s]
                        _, src, first_, blocks, _, _, _, ps = turns[n]
                        if n == 0:
                            pe.wait_ge(normed, A_UNITS)
                        elif n <= 2:
                            pe.wait_ge(normed, A_UNITS + B_UNITS)
                        elif n <= 6:
                            pe.wait_ge(rec_y, n - 2)
                            pe.wait_ge(normed, A_UNITS + B_UNITS)
                        else:
                            pe.wait_ge(summed, 4 + n - 6)
                            pe.wait_ge(kept, 4 * (LEVELS + 1))
                        if n:
                            pe.wait_ge(branch_lo, n)
                        for i in range(blocks):
                            for m in range(MT):
                                ins = pe.transpose(ps[:, i * T + m * P:i * T + (m + 1) * P],
                                                   src[:, m, (first_ + i) * P:(first_ + i + 1) * P], ident)
                        ins.then_inc(branch_turned, 1)

        with nc.Fori(0, DEPTH) as layer:
            with nc.Block() as block:
                layer_body(layer, block)
            for q in per_layer:
                nc.gpsimd.sem_clear(q)
            nc.all_engine_barrier()

        with nc.Block() as block:
            @block.sync
            def _(sp):
                sp.wait_ge(x_stored, 16 * (DEPTH + 1))


def constants():
    pos = np.arange(T, dtype=np.float32)
    freq = np.float32(THETA) ** (-np.arange(0, ROT, 2, dtype=np.float32) / np.float32(ROT))
    ang = (pos[:, None] * freq[None, :]).astype(np.float32)
    cos, sin = np.cos(ang), np.sin(ang)
    by_tile = lambda v: v.reshape(MT, P, ROT).transpose(1, 0, 2).reshape(P, MT * ROT)
    const = np.concatenate([np.eye(P, dtype=np.float32), by_tile(np.concatenate([cos, cos], 1)),
                            by_tile(np.concatenate([-sin, sin], 1))], 1).astype(np.float32)
    i = np.arange(T)
    rel = np.abs(i[:, None] - i[None, :])
    allowed = [(rel % dil == 0) & (rel // dil <= window // (2 * dil)) for window, dil in GROUPS] + [rel <= BWIN]
    masks = np.stack([np.where(a, 0.0, NEG) for a in allowed], 1).astype(np.float32)
    masks = masks.reshape(MT, P, (NG + 1) * T).transpose(1, 0, 2).reshape(P, -1)
    p = np.arange(P)
    levels = [((p[:, None] >> (l + 1)) == (p[None, :] >> (l + 1))) & ((p[:, None] >> l) != (p[None, :] >> l))
              for l in range(LEVELS - 1)]
    lmasks = np.stack(levels, 1).astype(np.float32).reshape(P, -1)
    return const, np.ascontiguousarray(masks), np.ascontiguousarray(lmasks)


def tiles(w):
    k, n = w.shape
    return w.reshape(k // (P * QK), QK, P, n // CW, CW).transpose(3, 0, 2, 1, 4)


W_IN_ORDER = [9, 0, 1, 2, 3, 4, 5, 6, 7, 8, 13, 14, 10, 11, 12, 15, 17, 19, 21, 23, 16, 18, 20, 22, 24]


def stream_of(w_in, w_a, w_b, w_c, w_out):
    t = tiles(w_in)
    parts = [t[c] for c in W_IN_ORDER]
    for b, w in enumerate((w_a, w_b, w_c)):
        z = tiles(w)
        for j in range(4):
            parts += [t[25 + 4 * b + j], z[j]]
    parts += list(tiles(w_out))
    return np.concatenate(parts, 0).reshape(NSTEPS, P, TILE)


def kernel(x, pre_norm, post_norm, w_in, sink_logits, hgrn_lower_bounds, hgrn_norm, w_branch_a, w_branch_b,
           w_branch_c, w_out):
    import concourse.bacc as bacc
    from concourse.bass_utils import run_bass_kernel_spmd

    x, pre_norm, post_norm, w_in, sink_logits, hgrn_lower_bounds, hgrn_norm, w_branch_a, w_branch_b, w_branch_c, w_out = (
        np.asarray(a) for a in (x, pre_norm, post_norm, w_in, sink_logits, hgrn_lower_bounds, hgrn_norm, w_branch_a,
                                w_branch_b, w_branch_c, w_out))
    const, masks, lmasks = constants()
    by_channel = lambda v: v.reshape(-1, P).T
    sel = [np.full((P, 1), float(layer > 0), np.float32) for layer in range(DEPTH)]
    par = np.stack([np.concatenate(
        [by_channel(pre_norm[n]), by_channel(hgrn_norm[n]), np.broadcast_to(sink_logits[n], (P, BQ)),
         by_channel(hgrn_lower_bounds.reshape(-1)), sel[n]], 1) for n in range(DEPTH)])
    weights = np.stack([stream_of(w_in[n], w_branch_a[n], w_branch_b[n], w_branch_c[n], w_out[n])
                        for n in range(DEPTH)])
    arrays = {"w_stream": weights, "x_in": x, "const_in": const, "masks_in": masks, "lmasks_in": lmasks,
              "params_in": np.ascontiguousarray(par), "post_in": post_norm}
    nc = bacc.Bacc("TRN2", target_bir_lowering=False, num_devices=1)
    aps = [nc.dram_tensor(n, a.shape, mybir.dt.from_np(a.dtype), kind="ExternalInput").ap() for n, a in arrays.items()]
    out = nc.dram_tensor("x_out", x.shape, F32, kind="ExternalOutput").ap()
    build(nc, *aps, out)
    r = run_bass_kernel_spmd(nc, [arrays], core_ids=[0])
    return r.results[0]["x_out"]
```

```python
from contextlib import ExitStack

import numpy as np

import concourse.bass as bass
from concourse import mybir

ALU = mybir.AluOpType
ACT = mybir.ActivationFunctionType
AX = mybir.AxisListType
F32 = mybir.dt.float32
F32R = mybir.dt.float32r
BF16 = mybir.dt.bfloat16
U8 = mybir.dt.uint8

P = 128
D = 2048
T = 256
MT = T // P
DEPTH = 2
KT = D // P
CW = 512
QK = 4
TILE = QK * CW
EPS = 1e-6
HD = 128
ROT = HD // 4
HALF = ROT // 2
THETA = 500000.0
SCALE = float(HD) ** -0.5
NEG = -1e30
GROUPS = ((128, 1), (512, 4), (2048, 16))
NG = len(GROUPS)
SLOTS = D // 512
BQ = D // 256
BKV = BQ // 4
BWIN = 128
CH = D // 256
LEVELS = 8
TINY = 1e-18
LN_TINY = float(-np.log(TINY))

CHUNKS = [("gate_a", 0, KT)]
CHUNKS += [("rope_qa", g, KT) for g in range(NG)] + [("rope_ka", g, KT) for g in range(NG)]
CHUNKS += [("v_a", g, KT) for g in range(NG)]
CHUNKS += [("gate_b", 0, KT), ("gate_b", 1, KT), ("rope_qb", 0, KT), ("rope_qb", 1, KT), ("rope_kv", 0, KT)]
for _g in range(2):
    CHUNKS += [(k, _g, KT) for k in ("c_q", "c_zf", "c_zb", "c_v", "gate_c")]
for _b, _k in (("a", SLOTS), ("b", BQ), ("c", CH)):
    for _j in range(4):
        CHUNKS += [("merge_" + _b, _j, KT), ("z_" + _b, _j, _k)]
CHUNKS += [("out", j, KT) for j in range(4)]

STEP_OF = []
STEPS = []
for _c, (_kind, _i, _k) in enumerate(CHUNKS):
    STEP_OF.append(len(STEPS))
    STEPS += [(_c, q) for q in range(_k // QK)]
NSTEPS = len(STEPS)
ENDS = {}
for _c, (_kind, _i, _k) in enumerate(CHUNKS):
    ENDS[STEP_OF[_c] + _k // QK - 1] = _c


def end_of(kind, i):
    c = [n for n, x in enumerate(CHUNKS) if x[:2] == (kind, i)][0]
    return STEP_OF[c] + CHUNKS[c][2] // QK - 1


TURNED = [c for c, x in enumerate(CHUNKS) if x[0].startswith("rope") or x[0] in ("c_q", "c_zf", "c_zb")]
ROPED = [c for c in TURNED if CHUNKS[c][0].startswith("rope")]
MERGES = [c for c, x in enumerate(CHUNKS) if x[0].startswith("merge")]

A_UNITS = SLOTS * MT
B_UNITS = BKV * MT
UNITS = [end_of("v_a", NG - 1) + 2 + 2 * u for u in range(A_UNITS)]
UNITS += [end_of("rope_kv", 0) + 3 + 2 * u for u in range(B_UNITS)]
TURN_A = UNITS[A_UNITS - 1] + 5
TURN_B = [UNITS[-1] + 6, UNITS[-1] + 8]
REC = [TURN_B[1] + 2 + 15 * u for u in range(4)]
FIRST_LEVEL = 7
Z_A_END = end_of("z_a", 3)
TURN_C = [Z_A_END + 3, Z_A_END + 5, Z_A_END + 7, REC[3] + FIRST_LEVEL + 11]
SP_EXTRA = TURN_C[3] + 3
assert TURN_C[3] + 2 < end_of("z_c", 0) and SP_EXTRA + 6 < STEP_OF[CHUNKS.index(("out", 0, KT))]
MASKS_AT = 7

SILUS = [c for c, x in enumerate(CHUNKS) if x[0].startswith("gate") or x[0] == "c_q"]
SPLIT = 1280
PIECE = D // 4
PARAMS = KT + CH + BQ + DEPTH * CH + 1


def build(nc, W, X, CONST, MASKS, LMASKS, PAR, POST, OUT):
    out_v = OUT.rearrange("b (m p) d -> p (b m) d", p=P)
    x_v = X.rearrange("b (m p) d -> p (b m) d", p=P)
    with ExitStack() as ctx:
        def sb(name, shape, dt=F32):
            return ctx.enter_context(nc.sbuf_tensor(name, shape, dt))

        def sem(name):
            return ctx.enter_context(nc.semaphore(name))

        K1 = 1024
        place = (nc.sbuf_base + 31) // 32 * 32
        sb("arena_fence", [P, 76 * K1 // 4 + 8])
        arena = nc.alloc_sbuf_tensor_at("arena", [P, 76 * K1 // 4], F32, offset=place)

        raw = sb("raw", [P, 2, TILE])
        w_hi = sb("w_hi", [P, 2, TILE], F32R)
        w_lo = sb("w_lo", [P, 2, TILE], F32R)
        xT_hi = sb("xT_hi", [P, KT, T], F32R)
        xT_lo = sb("xT_lo", [P, KT, T], F32R)
        aT_hi = sb("aT_hi", [P, 4, T], F32R)
        aT_lo = sb("aT_lo", [P, 4, T], F32R)
        bT_hi = sb("bT_hi", [P, BQ, T], F32R)
        bT_lo = sb("bT_lo", [P, BQ, T], F32R)
        stage = sb("stage", [P, MT, CW])
        wide = sb("wide", [P, 1028 + 1024])
        scores = wide[:, 0:1028]
        probsT = wide[:, 1028:2052]
        ropes = sb("ropes", [P, 2, MT * 4 * ROT])
        const = sb("const", [P, P + MT * ROT * 2])
        masks = sb("masks", [P, MT, (NG + 1) * T], BF16)
        lmasks = sb("lmasks", [P, LEVELS - 1, P], U8)
        par = sb("par", [P, PARAMS])
        lbs = sb("lbs", [P, 8, CH])
        small = sb("small", [P, 64])
        small2 = sb("small2", [P, 64])
        half_neg = sb("half_neg", [P, 1])
        def piece(at, shape, dt=F32):
            n = int(np.prod(shape))
            v = arena[:, at * K1 // 4: at * K1 // 4 + n]
            if len(shape) == 2:
                return v.rearrange("p (a b) -> p a b", b=shape[1])
            if len(shape) == 3:
                return v.rearrange("p (a b c) -> p a b c", b=shape[1], c=shape[2])
            return v

        qaT = piece(0, [NG * SLOTS, T])
        kaT = piece(12, [NG * SLOTS, T])
        va = piece(24, [NG, MT, CW])
        gate_a = piece(36, [MT, CW])
        qbT = piece(40, [BQ, T])
        kbT = piece(48, [BKV, T])
        vb = piece(50, [MT, BKV * HD])
        gate_b = piece(52, [2, MT, CW])
        cq = [piece(20 * g, [4, T]) for g in range(2)]
        cz = [[piece(20 * g + 4, [4, T]), piece(20 * g + 8, [4, T])] for g in range(2)]
        cv = [piece(20 * g + 12, [MT, CW]) for g in range(2)]
        gate_c = [piece(20 * g + 16, [MT, CW]) for g in range(2)]
        PI = piece(40, [2, 512])
        RX = piece(44, [2, 512])
        EQ = piece(48, [4, 512])
        S_diag = piece(56, [4, P])
        S_off = piece(58, [4, P])
        y = piece(60, [MT, D])
        x_sb = piece(40, [MT, D])
        ident = const[:, 0:P]
        cosT = const[:, P:P + MT * ROT].rearrange("p (m r) -> p m r", m=MT)
        sinT = const[:, P + MT * ROT:P + 2 * MT * ROT].rearrange("p (m r) -> p m r", m=MT)
        pre_gain = par[:, 0:KT]
        hg_gain = par[:, KT:KT + CH]
        sink = par[:, KT + CH:KT + CH + BQ]
        lb_raw = par[:, KT + CH + BQ:KT + CH + BQ + DEPTH * CH].rearrange("p (l h) -> p l h", l=DEPTH)
        lb_sel = par[:, PARAMS - 1:PARAMS]
        lb, one_lb, lb_tiny = lbs[:, 0], lbs[:, 1], lbs[:, 2]
        x_sumsq = small[:, 20:22]
        x_rstd = small[:, 22:24]
        half_rstd = small[:, 24:26]
        sumsq = small[:, 0:2]
        rstd = small[:, 2:4]
        out_sq = small[:, 4:12]
        rec_sq = small[:, 12:16]
        rec_rstd = small[:, 16:20]
        smax = small2[:, 0:8].rearrange("p (b i) -> p b i", b=2)
        nmax = small2[:, 8:16].rearrange("p (b i) -> p b i", b=2)
        dens = small2[:, 16:24].rearrange("p (b i) -> p b i", b=2)
        rden = small2[:, 24:32].rearrange("p (b i) -> p b i", b=2)
        post_gain = wide[:, 0:D]

        yT_hi = nc.alloc_sbuf_tensor_at("yT_hi", [P, KT, T], F32R, offset=place + 8 * K1)
        yT_lo = nc.alloc_sbuf_tensor_at("yT_lo", [P, KT, T], F32R, offset=place + 24 * K1)
        cT_hi = nc.alloc_sbuf_tensor_at("cT_hi", [P, 4, T], F32R, offset=place)
        cT_lo = nc.alloc_sbuf_tensor_at("cT_lo", [P, 4, T], F32R, offset=place + 4 * K1)

        acc = [ctx.enter_context(nc.psum_tensor(f"acc{i}", [P, MT * CW], F32)) for i in range(2)]
        side = [ctx.enter_context(nc.psum_tensor(f"side{i}", [P, MT * CW], F32)) for i in range(2)]
        accv = [a[:, :].rearrange("p (m c) -> p m c", m=MT) for a in acc]

        x_stored = sem("x_stored")
        const_landed = sem("const_landed")
        x_in = [sem(f"x_in{p}") for p in range(4)]
        first_landed = [sem(f"first_landed{i}") for i in range(3)]
        names = """w_landed0 w_landed1 acc_free0 acc_free1 par_landed masks_landed x_landed hi_ready lo_dve lo_pool
            pe_step dve_chain pool_chain x_squared x_rstd_ready x_turned xT_hi_ready xT_ready
            first_hi_ready staged roped turned tanhed scored masked probs probs_turned probs_copied attended
            normed branch_turned branch_hi branch_lo lb_ready rec_prep rec_exp rx_cleared logs_ready mixed grams
            decays scanned kept rec_out rec_squared rec_rstd_ready rec_y gated summed out_squared out_summed
            out_rstd y_scaled x_new x_new_pool""".split()
        (w_landed0, w_landed1, acc_free0, acc_free1, par_landed, masks_landed, x_landed, hi_ready, lo_dve, lo_pool,
         pe_step, dve_chain, pool_chain, x_squared, x_rstd_ready, x_turned, xT_hi_ready, xT_ready,
         first_hi_ready, staged, roped, turned, tanhed, scored, masked, probs, probs_turned, probs_copied, attended,
         normed, branch_turned, branch_hi, branch_lo, lb_ready, rec_prep, rec_exp, rx_cleared, logs_ready, mixed,
         grams, decays, scanned, kept, rec_out, rec_squared, rec_rstd_ready, rec_y, gated, summed, out_squared,
         out_summed, out_rstd, y_scaled, x_new, x_new_pool) = per_layer = [sem(n) for n in names]
        w_landed = [w_landed0, w_landed1]
        acc_free = [acc_free0, acc_free1]

        turns = [(TURN_A, gate_a, 0, 4, aT_hi[:, :, :], aT_lo[:, :, :], None, side[0][:, :])]
        for r in range(2):
            turns.append((TURN_B[r], gate_b[:, r], 0, 4, bT_hi[:, 4 * r:4 * r + 4], bT_lo[:, 4 * r:4 * r + 4],
                          None, side[0][:, :]))
        for u in range(4):
            g, j = u // 2, 2 * (u % 2)
            hi, lo = (aT_hi, aT_lo) if g == 0 else (cT_hi, cT_lo)
            turns.append((TURN_C[u], gate_c[g], j, 2, hi[:, j:j + 2, :], lo[:, j:j + 2, :],
                          hg_gain[:, 4 * g + j:4 * g + j + 2], side[1][:, 512:1024]))
        for j in range(4):
            turns.append((end_of("z_c", j) + 2, y[:, :, j * CW:(j + 1) * CW], 0, 4, yT_hi[:, 4 * j:4 * j + 4, :],
                          yT_lo[:, 4 * j:4 * j + 4, :], None, side[j % 2][:, :]))
        TURN_AT = {t[0]: n for n, t in enumerate(turns)}

        def lhs(c, k):
            kind = CHUNKS[c][0]
            if kind == "out":
                return yT_hi[:, k, :], yT_lo[:, k, :]
            if kind == "z_a" or (kind == "z_c" and k < 4):
                return aT_hi[:, k, :], aT_lo[:, k, :]
            if kind == "z_b":
                return bT_hi[:, k, :], bT_lo[:, k, :]
            if kind == "z_c":
                return cT_hi[:, k - 4, :], cT_lo[:, k - 4, :]
            return xT_hi[:, k, :], xT_lo[:, k, :]

        def halves(v, level):
            w = v.rearrange("p (n two l) -> p n two l", two=2, l=1 << level)
            return w[:, :, 0, :], w[:, :, 1, :]

        def unit(u):
            if u < A_UNITS:
                h, m = divmod(u, MT)
                q = [qaT[:, g * SLOTS + h, m * P:(m + 1) * P] for g in range(NG)]
                k = [kaT[:, g * SLOTS + h, :] for g in range(NG)]
                return q, k, m
            kv, m = divmod(u - A_UNITS, MT)
            q = [qbT[:, 4 * kv + i, m * P:(m + 1) * P] for i in range(4)]
            return q, [kbT[:, kv, :]] * 4, m

        def rec_views(u):
            g, j = u // 2, 2 * (u % 2)
            flat = lambda v: v[:, j:j + 2, :].rearrange("p h t -> p (h t)")
            return flat(cq[g]), [flat(z) for z in cz[g]], cv[g], gate_c[g], 4 * g + j, j

        def columns(v, p):
            return v[:, :, p * PIECE:(p + 1) * PIECE]

        def x_blocks(b):
            return (acc[0], acc[1], side[0], side[1])[b // 2][:, (b % 2) * 512:(b % 2) * 512 + 512]

        def turn_x(pe, p):
            for b in (2 * p, 2 * p + 1):
                for m in range(MT):
                    for i in range(2):
                        k = 2 * b + i
                        ins = pe.transpose(x_blocks(b)[:, i * T + m * P:i * T + (m + 1) * P], x_sb[:, m, k * P:(k + 1) * P],
                                           ident)
            ins.then_inc(x_turned, 1)

        def split_x_hi(act, b, done):
            for i in range(2):
                k = 2 * b + i
                ins = act.activation(xT_hi[:, k, :], x_blocks(b)[:, i * T:(i + 1) * T], ACT.Copy, scale=pre_gain[:, k:k + 1])
            ins.then_inc(done, 1)

        def split_x_lo(dve, b, done):
            for i in range(2):
                k = 2 * b + i
                ins = dve.scalar_tensor_tensor(out=xT_lo[:, k, :], in0=x_blocks(b)[:, i * T:(i + 1) * T],
                                               scalar=pre_gain[:, k:k + 1], in1=xT_hi[:, k, :].bitcast(F32),
                                               op0=ALU.mult, op1=ALU.subtract)
            ins.then_inc(done, 1)

        def w_hi_of(act, s):
            return act.activation(w_hi[:, s % 2, :], raw[:, s % 2, :], ACT.Copy)

        def w_lo_of(eng, s, cols):
            return eng.tensor_tensor(w_lo[:, s % 2, cols], raw[:, s % 2, cols], w_hi[:, s % 2, cols].bitcast(F32),
                                     ALU.subtract)

        DVE_COLS, POOL_COLS = slice(0, SPLIT), slice(SPLIT, TILE)

        def counts_from_zero():
            numbers = [q.num for q in per_layer]
            assert numbers == list(range(numbers[0], numbers[0] + len(numbers)))
            nc.gpsimd.sem_clear(range(numbers[0], numbers[-1] + 1))
            nc.all_engine_barrier()

        with nc.Block() as block:
            @block.sync
            def _(sp):
                sp.dma_start(columns(x_sb, 0), columns(x_v, 0)).then_inc(x_in[0], 16)
                sp.dma_start(raw[:, 0, :], W[0]).then_inc(first_landed[0], 16)
                for p in range(1, 4):
                    sp.dma_start(columns(x_sb, p), columns(x_v, p)).then_inc(x_in[p], 16)
                sp.dma_start(raw[:, 1, :], W[1]).then_inc(first_landed[1], 16)
                sp.wait_ge(lo_dve, 1)
                sp.wait_ge(lo_pool, 1)
                sp.dma_start(raw[:, 0, :], W[2]).then_inc(first_landed[2], 16)
                for p in range(4):
                    sp.wait_ge(x_in[p], 16)
                    sp.dma_start(columns(out_v, p), columns(x_sb, p)).then_inc(x_stored, 16)

            @block.gpsimd
            def _(pool):
                pool.memset(half_neg[:, :], -0.5)
                pool.wait_ge(hi_ready, 1)
                w_lo_of(pool, 0, POOL_COLS).then_inc(lo_pool, 1)

            @block.scalar
            def _(act):
                act.dma_start(const[:, :], CONST).then_inc(const_landed, 16)
                act.dma_start(par[:, :], PAR[0]).then_inc(par_landed, 16)
                act.wait_ge(par_landed, 16)
                act.wait_ge(x_turned, 1)
                for b in range(2):
                    split_x_hi(act, b, first_hi_ready)
                act.wait_ge(first_landed[0], 16)
                w_hi_of(act, 0).then_inc(hi_ready, 1)

            @block.vector
            def _(dve):
                for b in range(2):
                    dve.wait_ge(first_hi_ready, b + 1)
                    split_x_lo(dve, b, xT_ready)
                dve.wait_ge(hi_ready, 1)
                w_lo_of(dve, 0, DVE_COLS).then_inc(lo_dve, 1)

            @block.tensor
            def _(pe):
                pe.wait_ge(const_landed, 16)
                for p in range(4):
                    pe.wait_ge(x_in[p], 16)
                    turn_x(pe, p)
        counts_from_zero()

        def evacuated(eng, c):
            eng.wait_ge(acc_free[c % 2], c // 2 + 1)

        def layer_body(layer, block):
            @block.sync
            def _(sp):
                for s in range(3, NSTEPS + 3):
                    sp.wait_ge(lo_dve, s - 2)
                    sp.wait_ge(lo_pool, s - 2)
                    landed = w_landed[s % 2] if s < NSTEPS else first_landed[s - NSTEPS]
                    sp.dma_start(raw[:, s % 2, :], W[layer * NSTEPS + s]).then_inc(landed, 16)
                    if s == 3:
                        sp.dma_start(y[:, 0, 0:MT * (NG + 1) * T],
                                     MASKS).then_inc(masks_landed, 16)
                        sp.dma_start(y[:, 1, 0:(LEVELS - 1) * P], LMASKS).then_inc(masks_landed, 16)
                    p = s - SP_EXTRA
                    if 0 <= p < 4:
                        if p == 0:
                            sp.wait_ge(x_stored, 64 * (layer + 1))
                            sp.wait_ge(branch_lo, 7)
                        sp.dma_start(columns(x_sb, p), columns(out_v, p)).then_inc(x_landed, 16)
                    if p == 4:
                        sp.dma_start(post_gain, POST[layer].partition_broadcast(P)).then_inc(x_landed, 16)
                        sp.dma_start(par[:, :], PAR[layer + 1]).then_inc(par_landed, 16)
                for p in range(4):
                    if p == 0:
                        sp.wait_ge(x_landed, 80)
                    if p < 3:
                        sp.wait_ge(x_new, p + 1)
                    else:
                        sp.wait_ge(x_new_pool, 1)
                    sp.dma_start(columns(out_v, p), columns(x_sb, p)).then_inc(x_stored, 16)

            @block.gpsimd
            def _(pool):
                count = [0]

                def link(ins):
                    count[0] += 1
                    ins.then_inc(pool_chain, 1)
                    pool.wait_ge(pool_chain, count[0])

                def lo(s):
                    pool.wait_ge(hi_ready, s)
                    if s >= 2:
                        pool.wait_ge(pe_step, s - 1)
                    w_lo_of(pool, s, POOL_COLS).then_inc(lo_pool, 1)

                def power(dst, src, mean):
                    n = src.shape[1]
                    link(pool.tensor_scalar(dst, src, mean, EPS, ALU.mult, ALU.add))
                    return pool.tensor_tensor(dst, dst, half_neg[:, :].broadcast_to([P, n]), ALU.pow)

                for s in range(NSTEPS + 3):
                    if s < NSTEPS:
                        lo(s + 1)
                    if s == 3:
                        pool.wait_ge(x_squared, 2)
                        link(power(x_rstd, x_sumsq, 1.0 / D))
                        pool.tensor_scalar(half_rstd, x_rstd, 0.5, None, ALU.mult).then_inc(x_rstd_ready, 1)
                    for u in range(4):
                        if s == REC[u] + 5:
                            pool.wait_ge(rec_prep, 2 * u + 2)
                            pool.memset(RX, 0.0).then_inc(rx_cleared, 1)
                        l = s - REC[u] - FIRST_LEVEL
                        if 0 <= l < LEVELS - 1:
                            pool.wait_ge(decays, LEVELS * u + l + 1)
                            pf_lo, pf_up = halves(PI[:, 0], l)
                            rx_lo, _ = halves(RX[:, 0], l)
                            pb_lo, pb_up = halves(PI[:, 1], l)
                            _, rb_up = halves(RX[:, 1], l)
                            n, L = 512 >> (l + 1), 1 << l
                            last = lambda v: v[:, :, L - 1:L].broadcast_to([P, n, L])
                            head = lambda v: v[:, :, 0:1].broadcast_to([P, n, L])
                            pool.tensor_tensor(rx_lo, rx_lo, last(pf_up), ALU.add)
                            link(pool.tensor_tensor(rb_up, rb_up, head(pb_lo), ALU.add))
                            pool.tensor_tensor(pf_up, pf_up, last(pf_lo), ALU.add)
                            link(pool.tensor_tensor(pb_lo, pb_lo, head(pb_up), ALU.add))
                            pool.nop().then_inc(scanned, 1)
                        if s == REC[u] + FIRST_LEVEL + 9:
                            pool.wait_ge(rec_squared, u + 1)
                            link(power(rec_rstd, rec_sq, 1.0 / HD))
                            by_tile = lambda v: v.rearrange("p (h m) -> p h m", m=MT)
                            pool.tensor_tensor(by_tile(rec_rstd), by_tile(rec_rstd),
                                               x_rstd[:, None, :].broadcast_to([P, 2, MT]),
                                               ALU.mult).then_inc(rec_rstd_ready, 1)
                    for late, kind in ((2, "z_b"), (1, "z_c")):
                        c = ENDS.get(s - late)
                        if c is None or CHUNKS[c][0] != kind:
                            continue
                        n = [x for x in range(c + 1) if CHUNKS[x][0] in ("z_b", "z_c")]
                        j = CHUNKS[c][1]
                        pool.wait_ge(gated, len(n) + 4)
                        part = y[:, :, j * CW:(j + 1) * CW]
                        pool.tensor_tensor(part, part, stage[:, :, :], ALU.add).then_inc(summed, 1)
                pool.wait_ge(out_summed, 1)
                power(rstd, sumsq, 1.0 / D).then_inc(out_rstd, 1)
                pool.wait_ge(x_landed, 80)
                pool.wait_ge(y_scaled, 1)
                pool.tensor_tensor(columns(x_sb, 3), columns(x_sb, 3), columns(y, 3), ALU.add).then_inc(x_new_pool, 1)

            @block.scalar
            def _(act):
                def hi(s):
                    if s < 3:
                        act.wait_ge(first_landed[s], 16 * (layer + 1))
                    elif s == NSTEPS:
                        act.wait_ge(first_landed[0], 16 * (layer + 2))
                    else:
                        act.wait_ge(w_landed[s % 2], 16 * ((s - 1) // 2))
                    if s >= 2:
                        act.wait_ge(pe_step, s - 1)
                    w_hi_of(act, s).then_inc(hi_ready, 1)

                def scaled(dst, src, func, scale, done=None):
                    for m in range(MT):
                        ins = act.activation(dst[:, m], src[:, m], func, scale=scale[:, m:m + 1])
                    if done is not None:
                        ins.then_inc(done, 1)

                for s in range(NSTEPS + 3):
                    if s < NSTEPS:
                        hi(s + 1)
                    if s == 0:
                        for b in range(2, KT // 2):
                            split_x_hi(act, b, xT_hi_ready)
                    if s in (1, 2):
                        if s == 2:
                            act.wait_ge(x_squared, 1)
                        act.activation(wide[:, 0:D], x_sb[:, s - 1, :], ACT.Square,
                                       accum_out=x_sumsq[:, s - 1:s]).then_inc(x_squared, 1)
                    if s == 3:
                        act.wait_ge(lb_ready, 1)
                        act.activation(lbs[:, 4:4 + DEPTH, :], lbs[:, 4:4 + DEPTH, :], ACT.Exp).then_inc(lb_ready, 1)
                        act.wait_ge(x_rstd_ready, 1)
                    c = ENDS.get(s - 1)
                    if c is not None:
                        kind, i, _ = CHUNKS[c]
                        act.wait_ge(pe_step, s)
                        if c in TURNED:
                            n = TURNED.index(c)
                            if n:
                                act.wait_ge(turned, n)
                            if kind == "rope_kv":
                                scaled(vb, accv[c % 2][:, :, T:2 * T], ACT.Copy, x_rstd)
                                scaled(stage[:, :, 0:T], accv[c % 2][:, :, 0:T], ACT.Copy, x_rstd, staged)
                            else:
                                scaled(stage, accv[c % 2], ACT.Copy, x_rstd, staged)
                        elif kind in ("v_a", "c_v"):
                            if kind == "c_v":
                                act.wait_ge(branch_turned, 1)
                            scaled(va[:, i] if kind == "v_a" else cv[i], accv[c % 2], ACT.Copy, x_rstd, acc_free[c % 2])
                        elif kind.startswith("gate"):
                            dst = {"gate_a": lambda: gate_a, "gate_b": lambda: gate_b[:, i],
                                   "gate_c": lambda: gate_c[i]}[kind]()
                            if kind == "gate_b" and i == 0:
                                act.wait_ge(x_stored, 64 * (layer + 1))
                            if kind == "gate_c":
                                act.wait_ge(branch_turned, 1)
                            scaled(dst, accv[c % 2], ACT.Tanh, half_rstd, tanhed)
                        elif kind.startswith("merge"):
                            n = MERGES.index(c)
                            if n == 0:
                                act.wait_ge(turned, len(TURNED))
                            elif n <= 4:
                                act.wait_ge(gated, n)
                            else:
                                act.wait_ge(summed, n - 4)
                            scaled(stage, accv[c % 2], ACT.Tanh, half_rstd, acc_free[c % 2])
                        elif kind == "out":
                            act.wait_ge(summed, 8)
                            if i:
                                act.wait_ge(out_squared, 2 * i)
                            for m in range(MT):
                                act.activation(stage[:, m, :], accv[c % 2][:, m, :], ACT.Square,
                                               accum_out=out_sq[:, 4 * m + i:4 * m + i + 1]).then_inc(out_squared, 1)
                    c = ENDS.get(s - 2)
                    if c is not None and CHUNKS[c][0] in ("c_q", "c_zf", "c_zb"):
                        kind, i, _ = CHUNKS[c]
                        act.wait_ge(turned, TURNED.index(c) + 1)
                        act.wait_ge(branch_turned, 1)
                        src = acc[c % 2][:, :].rearrange("p (h t) -> p h t", h=4)
                        if kind == "c_q":
                            act.activation(cq[i], src, ACT.Tanh, scale=0.5).then_inc(tanhed, 1)
                        else:
                            act.activation(cz[i][kind == "c_zb"], src, ACT.Copy).then_inc(acc_free[c % 2], 1)
                    c = ENDS.get(s - 3)
                    if c is not None and c in ROPED:
                        kind, i, _ = CHUNKS[c]
                        act.wait_ge(turned, TURNED.index(c) + 1)
                        dst = {"rope_qa": qaT, "rope_ka": kaT, "rope_qb": qbT, "rope_kv": kbT}[kind]
                        if kind != "rope_kv":
                            dst = dst[:, 4 * i:4 * i + 4]
                        nh = dst.shape[1]
                        act.activation(dst, acc[c % 2][:, 0:nh * T].rearrange("p (h t) -> p h t", h=nh),
                                       ACT.Copy).then_inc(acc_free[c % 2], 1)
                    for u, s0 in enumerate(UNITS):
                        if s == s0 + 2:
                            act.wait_ge(masked, u + 1)
                            b = u % 2
                            if u < A_UNITS:
                                act.activation(scores[:, 0:NG * T], scores[:, 0:NG * T], ACT.Exp, bias=nmax[:, b, 0:1],
                                               scale=SCALE, accum_out=dens[:, b, 0:1]).then_inc(probs, 1)
                            else:
                                for i in range(4):
                                    v = scores[:, 257 * i:257 * i + 257]
                                    ins = act.activation(v, v, ACT.Exp, bias=nmax[:, b, i:i + 1], scale=SCALE,
                                                         accum_out=dens[:, b, i:i + 1])
                                    if i == 3:
                                        ins.then_inc(probs, 1)
                        if s == s0 + 3:
                            act.wait_ge(probs_turned, u + 1)
                            if u:
                                act.wait_ge(attended, u)
                            n = NG * T if u < A_UNITS else 4 * T
                            act.activation(probsT[:, 0:n], side[1][:, 0:n], ACT.Copy).then_inc(probs_copied, 1)
                    if s - 1 in TURN_AT:
                        n = TURN_AT[s - 1]
                        _, _, _, blocks, dst, _, gain, ps = turns[n]
                        act.wait_ge(branch_turned, n + 1)
                        src = ps.rearrange("p (i t) -> p i t", t=T)
                        if gain is None:
                            act.activation(dst, src, ACT.Copy, scale=0.5).then_inc(branch_hi, 1)
                        else:
                            for i in range(blocks):
                                ins = act.activation(dst[:, i], src[:, i], ACT.Copy, scale=gain[:, i:i + 1])
                            ins.then_inc(branch_hi, 1)
                    for u in range(4):
                        d = s - REC[u]
                        if d == 1:
                            act.wait_ge(rec_prep, 2 * u + 1)
                            act.activation(EQ, EQ, ACT.Exp).then_inc(rec_exp, 1)
                        if d == 5:
                            act.wait_ge(rec_prep, 2 * u + 2)
                            act.activation(EQ[:, 0:2], EQ[:, 0:2], ACT.Ln).then_inc(rec_exp, 1)
                        l = d - FIRST_LEVEL
                        if 0 <= l < LEVELS:
                            if l == 0:
                                act.wait_ge(logs_ready, u + 1)
                                act.wait_ge(rx_cleared, u + 1)
                            act.wait_ge(mixed, (LEVELS + 1) * u + l + 1)
                            if l:
                                act.wait_ge(scanned, (LEVELS - 1) * u + l)
                            ef_lo, ef_up = halves(EQ[:, 0], l)
                            eb_lo, eb_up = halves(EQ[:, 1], l)
                            act.activation(ef_up, halves(PI[:, 0], l)[1], ACT.Exp)
                            act.activation(ef_lo, halves(RX[:, 0], l)[0], ACT.Exp)
                            act.activation(eb_lo, halves(PI[:, 1], l)[0], ACT.Exp)
                            act.activation(eb_up, halves(RX[:, 1], l)[1], ACT.Exp).then_inc(decays, 1)
                        if d == FIRST_LEVEL + 9:
                            act.wait_ge(rec_out, u + 1)
                            for i in range(4):
                                ins = act.activation(wide[:, i * P:(i + 1) * P], side[1][:, i * P:(i + 1) * P], ACT.Square,
                                                     scale=0.5, accum_out=rec_sq[:, i:i + 1])
                            ins.then_inc(rec_squared, 1)
                act.wait_ge(out_rstd, 1)
                evacuated(act, len(CHUNKS) - 1)
                scaled(columns(y, 3), columns(y, 3), ACT.Copy, rstd, y_scaled)
                act.wait_ge(par_landed, 16)
                act.wait_ge(x_turned, 1)
                for b in range(2):
                    split_x_hi(act, b, first_hi_ready)

            @block.vector
            def _(dve):
                count = [0]

                def link(ins):
                    count[0] += 1
                    ins.then_inc(dve_chain, 1)
                    dve.wait_ge(dve_chain, count[0])

                def lo(s):
                    dve.wait_ge(hi_ready, s)
                    if s >= 2:
                        dve.wait_ge(pe_step, s - 1)
                    w_lo_of(dve, s, DVE_COLS).then_inc(lo_dve, 1)

                def lower_bounds():
                    link(dve.tensor_tensor(lbs[:, 3], lb_raw[:, 0], lb_raw[:, 1], ALU.max))
                    dve.tensor_tensor(lbs[:, 4], lb_raw[:, 0], lbs[:, 3], ALU.subtract)
                    dve.tensor_tensor(lbs[:, 5], lb_raw[:, 1], lbs[:, 3], ALU.subtract).then_inc(lb_ready, 1)
                    dve.tensor_scalar(hg_gain, hg_gain, 0.25, None, ALU.mult)
                    dve.tensor_scalar(sink, sink, 1.0 / SCALE, None, ALU.mult)
                    dve.wait_ge(lb_ready, 2)
                    link(dve.tensor_tensor(lbs[:, 6], lbs[:, 4], lbs[:, 5], ALU.add))
                    link(dve.reciprocal(lbs[:, 6], lbs[:, 6]))
                    link(dve.tensor_tensor(lbs[:, 6], lbs[:, 6], lbs[:, 5], ALU.mult))
                    link(dve.tensor_scalar(lb, lbs[:, 6], lb_sel, None, ALU.mult))
                    dve.tensor_scalar(one_lb, lb, -1.0, 1.0, ALU.mult, ALU.add)
                    link(dve.tensor_scalar(lb_tiny, lb, TINY, None, ALU.is_lt))

                def rope(c, n):
                    dve.wait_ge(staged, TURNED.index(c) + 1)
                    st = stage[:, :, 0:n * HD].rearrange("p m (h d) -> p m h d", d=HD)
                    ta = ropes[:, 0, 0:MT * n * ROT].rearrange("p (m h r) -> p m h r", m=MT, h=n)
                    tb = ropes[:, 1, 0:MT * n * ROT].rearrange("p (m h r) -> p m h r", m=MT, h=n)
                    wide_ = lambda v, w: v[:, :, None, :].broadcast_to([P, MT, n, w])
                    dve.tensor_tensor(ta, st[:, :, :, 0:ROT], wide_(cosT, ROT), ALU.mult)
                    dve.tensor_tensor(tb[:, :, :, 0:HALF], st[:, :, :, HALF:ROT], wide_(sinT[:, :, 0:HALF], HALF), ALU.mult)
                    link(dve.tensor_tensor(tb[:, :, :, HALF:ROT], st[:, :, :, 0:HALF], wide_(sinT[:, :, HALF:ROT], HALF),
                                           ALU.mult))
                    dve.tensor_tensor(st[:, :, :, 0:ROT], ta, tb, ALU.add).then_inc(roped, 1)

                for s in range(NSTEPS + 3):
                    if s < NSTEPS:
                        lo(s + 1)
                    if s == 0:
                        for b in range(2, KT // 2):
                            dve.wait_ge(xT_hi_ready, b - 1)
                            split_x_lo(dve, b, xT_ready)
                    if s == 3:
                        lower_bounds()
                    if s == MASKS_AT:
                        dve.wait_ge(masks_landed, 32)
                        dve.tensor_copy(masks[:, :, :].rearrange("p m c -> p (m c)"),
                                        y[:, 0, 0:MT * (NG + 1) * T])
                    if s == MASKS_AT + 1:
                        dve.tensor_copy(lmasks[:, :, :].rearrange("p l c -> p (l c)"), y[:, 1, 0:(LEVELS - 1) * P])
                    for u in range(4):
                        d = s - REC[u]
                        q, z, _, gate, head, j = rec_views(u)
                        nine = (LEVELS + 1) * u
                        if d == 0:
                            if u == 0:
                                dve.wait_ge(branch_turned, 3)
                            else:
                                dve.wait_ge(grams, nine)
                            evacuated(dve, CHUNKS.index(("c_zb", u // 2, KT)))
                            for x in range(2):
                                dve.tensor_scalar(EQ[:, x], z[x], 0.0, None, ALU.min)
                                dve.tensor_scalar(EQ[:, 2 + x], z[x], -1.0, 0.0, ALU.mult, ALU.min)
                                ins = dve.tensor_scalar(PI[:, x], z[x], LN_TINY, 0.0, ALU.add, ALU.min)
                            ins.then_inc(rec_prep, 1)
                        if d == 2:
                            dve.wait_ge(rec_exp, 2 * u + 1)
                            link(dve.tensor_tensor(RX, EQ[:, 0:2], EQ[:, 2:4], ALU.add))
                            dve.reciprocal(RX[:, 0], RX[:, 0])
                        if d == 3:
                            dve.reciprocal(RX[:, 1], RX[:, 1])
                            for x in range(2):
                                for h in range(2):
                                    cols = slice(h * T, (h + 1) * T)
                                    ins = dve.scalar_tensor_tensor(
                                        out=EQ[:, x, cols], in0=EQ[:, 2 + x, cols], scalar=lb[:, head + h:head + h + 1],
                                        in1=EQ[:, x, cols], op0=ALU.mult, op1=ALU.add)
                            link(ins)
                        if d == 4:
                            link(dve.tensor_tensor(EQ[:, 0:2], EQ[:, 0:2], RX, ALU.mult))
                            for x in range(2):
                                for h in range(2):
                                    cols = slice(h * T, (h + 1) * T)
                                    ins = dve.scalar_tensor_tensor(
                                        out=z[x][:, cols], in0=EQ[:, 2 + x, cols], scalar=one_lb[:, head + h:head + h + 1],
                                        in1=RX[:, x, cols], op0=ALU.mult, op1=ALU.mult)
                            link(ins)
                            dve.tensor_scalar(EQ[:, 0:2], EQ[:, 0:2], TINY, None, ALU.max).then_inc(rec_prep, 1)
                            dve.tensor_tensor(EQ[:, 2], z[0], z[1], ALU.add).then_inc(mixed, 1)
                        if d == 6:
                            dve.wait_ge(rec_exp, 2 * u + 2)
                            for x in range(2):
                                for h in range(2):
                                    cols = slice(h * T, (h + 1) * T)
                                    ins = dve.scalar_tensor_tensor(
                                        out=PI[:, x, cols], in0=PI[:, x, cols], scalar=lb_tiny[:, head + h:head + h + 1],
                                        in1=EQ[:, x, cols], op0=ALU.mult, op1=ALU.add)
                            ins.then_inc(logs_ready, 1)
                        l = d - FIRST_LEVEL
                        if 0 <= l < LEVELS:
                            dve.wait_ge(grams, nine + l + 1)
                            src = side[0][:, (nine + l) % 2 * 512:(nine + l) % 2 * 512 + 512].rearrange(
                                "p (b t) -> p b t", t=P)
                            if l == 0:
                                if u:
                                    dve.wait_ge(rec_out, u)
                                ins = dve.tensor_copy(S_diag, src)
                            else:
                                dve.wait_ge(kept, nine + l)
                                ins = dve.copy_predicated(S_diag, lmasks[:, l - 1:l, :].broadcast_to([P, 4, P]), src)
                            ins.then_inc(kept, 1)
                            dve.wait_ge(decays, LEVELS * u + l + 1)
                            (ef_lo, ef_up), (eb_lo, eb_up) = halves(EQ[:, 0], l), halves(EQ[:, 1], l)
                            (k_lo, k_up), (q_lo, q_up) = halves(EQ[:, 2], l), halves(EQ[:, 3], l)
                            dve.tensor_tensor(k_lo, halves(z[0], l)[0], ef_lo, ALU.mult)
                            dve.tensor_tensor(k_up, halves(z[1], l)[1], eb_up, ALU.mult)
                            dve.tensor_tensor(q_up, halves(q, l)[1], ef_up, ALU.mult)
                            dve.tensor_tensor(q_lo, halves(q, l)[0], eb_lo, ALU.mult).then_inc(mixed, 1)
                        if d == FIRST_LEVEL + 8:
                            dve.wait_ge(grams, nine + LEVELS + 1)
                            dve.tensor_copy(S_off, side[0][:, (nine + LEVELS) % 2 * 512:(nine + LEVELS) % 2 * 512 + 512]
                                            .rearrange("p (b t) -> p b t", t=P)).then_inc(kept, 1)
                        if d == FIRST_LEVEL + 10:
                            dve.wait_ge(rec_rstd_ready, u + 1)
                            evacuated(dve, CHUNKS.index(("gate_c", u // 2, KT)))
                            for h in range(2):
                                for m in range(MT):
                                    i = h * MT + m
                                    part = gate[:, m, (j + h) * HD:(j + h + 1) * HD]
                                    ins = dve.scalar_tensor_tensor(out=part, in0=side[1][:, i * P:(i + 1) * P],
                                                                   scalar=rec_rstd[:, i:i + 1], in1=part,
                                                                   op0=ALU.mult, op1=ALU.mult)
                            ins.then_inc(rec_y, 1)
                    for u, s0 in enumerate(UNITS):
                        b = u % 2
                        m = unit(u)[2]
                        nh = 1 if u < A_UNITS else 4
                        if s == s0 + 1:
                            dve.wait_ge(scored, u + 1)
                            if u:
                                dve.wait_ge(probs_turned, u)
                            if u < A_UNITS:
                                v = scores[:, 0:NG * T]
                                link(dve.tensor_tensor(v, side[0][:, 0:NG * T], masks[:, m, 0:NG * T], ALU.add))
                                link(dve.reduce_max(smax[:, b, 0:1], v, AX.X))
                            else:
                                v = scores.rearrange("p (i t) -> p i t", i=4)
                                kv = (u - A_UNITS) // MT
                                dve.tensor_copy(v[:, :, T], sink[:, 4 * kv:4 * kv + 4])
                                link(dve.tensor_tensor(v[:, :, 0:T], side[0][:, :].rearrange("p (i t) -> p i t", i=4),
                                                       masks[:, m:m + 1, NG * T:(NG + 1) * T].broadcast_to([P, 4, T]), ALU.add))
                                link(dve.reduce_max(smax[:, b, :], v, AX.X))
                            dve.tensor_scalar(nmax[:, b, 0:nh], smax[:, b, 0:nh], -SCALE, None, ALU.mult).then_inc(masked, 1)
                        if s == s0 + 3:
                            dve.wait_ge(probs, u + 1)
                            link(dve.reciprocal(rden[:, b, 0:nh], dens[:, b, 0:nh]))
                            link(dve.tensor_scalar(rden[:, b, 0:nh], rden[:, b, 0:nh], x_rstd[:, m:m + 1], None, ALU.mult))
                        if s == s0 + 4:
                            dve.wait_ge(attended, u + 1)
                            for i in range(nh):
                                if u < A_UNITS:
                                    if u == 0:
                                        evacuated(dve, 0)
                                    h = u // MT
                                    part = gate_a[:, m, h * HD:(h + 1) * HD]
                                else:
                                    part = gate_b[:, (u - A_UNITS) // MT, m, i * HD:(i + 1) * HD]
                                ins = dve.scalar_tensor_tensor(out=part, in0=side[1][:, i * P:(i + 1) * P],
                                                               scalar=rden[:, b, i:i + 1], in1=part,
                                                               op0=ALU.mult, op1=ALU.mult)
                            ins.then_inc(normed, 1)
                    if s - 1 in TURN_AT:
                        n = TURN_AT[s - 1]
                        _, _, _, blocks, hi_, lo_, gain, ps = turns[n]
                        dve.wait_ge(branch_hi, n + 1)
                        src = ps.rearrange("p (i t) -> p i t", t=T)
                        if gain is None:
                            dve.scalar_tensor_tensor(out=lo_, in0=src, scalar=0.5, in1=hi_.bitcast(F32), op0=ALU.mult,
                                                     op1=ALU.subtract).then_inc(branch_lo, 1)
                        else:
                            for i in range(blocks):
                                ins = dve.scalar_tensor_tensor(out=lo_[:, i], in0=src[:, i], scalar=gain[:, i:i + 1],
                                                               in1=hi_[:, i].bitcast(F32), op0=ALU.mult, op1=ALU.subtract)
                            ins.then_inc(branch_lo, 1)
                    c = ENDS.get(s - 1)
                    if c is not None and CHUNKS[c][0].startswith("z_"):
                        kind, j, _ = CHUNKS[c]
                        dve.wait_ge(pe_step, s)
                        evacuated(dve, c - 1)
                        dst = y[:, :, j * CW:(j + 1) * CW] if kind == "z_a" else stage[:, :, :]
                        dve.scalar_tensor_tensor(out=dst, in0=stage[:, :, :], scalar=1.0, in1=accv[c % 2], op0=ALU.add,
                                                 op1=ALU.mult).then_inc(gated, 1)
                        dve.wait_ge(gated, (c - CHUNKS.index(("merge_a", 0, KT)) + 1) // 2)
                        dve.nop().then_inc(acc_free[c % 2], 1)
                    c = ENDS.get(s - 2)
                    if c is not None:
                        kind, i, _ = CHUNKS[c]
                        if kind.startswith("rope"):
                            rope(c, 2 if kind == "rope_kv" else 4)
                        if kind.startswith("gate"):
                            dve.wait_ge(tanhed, SILUS.index(c) + 1)
                            dst = {"gate_a": lambda: gate_a, "gate_b": lambda: gate_b[:, i],
                                   "gate_c": lambda: gate_c[i]}[kind]()
                            dve.scalar_tensor_tensor(out=dst, in0=dst, scalar=1.0, in1=accv[c % 2], op0=ALU.add,
                                                     op1=ALU.mult).then_inc(acc_free[c % 2], 1)
                        if kind == "out":
                            dve.wait_ge(branch_turned, 8 + i)
                            if i == 0:
                                dve.wait_ge(x_landed, 80)
                            for m in range(MT):
                                dve.wait_ge(out_squared, 2 * i + m + 1)
                                if i == 3 and m == MT - 1:
                                    dve.tensor_reduce(sumsq, out_sq.rearrange("p (m j) -> p m j", m=MT), AX.X,
                                                      ALU.add).then_inc(out_summed, 1)
                                ins = dve.tensor_tensor(y[:, m, i * CW:(i + 1) * CW], accv[c % 2][:, m],
                                                        post_gain[:, i * CW:(i + 1) * CW], ALU.mult)
                            ins.then_inc(acc_free[c % 2], 1)
                    c = ENDS.get(s - 3)
                    if c is not None and CHUNKS[c][0] == "c_q":
                        dve.wait_ge(tanhed, SILUS.index(c) + 1)
                        dst = cq[CHUNKS[c][1]]
                        dve.scalar_tensor_tensor(out=dst, in0=dst, scalar=1.0,
                                                 in1=acc[c % 2][:, :].rearrange("p (h t) -> p h t", h=4),
                                                 op0=ALU.add, op1=ALU.mult).then_inc(acc_free[c % 2], 1)
                dve.wait_ge(out_rstd, 1)
                evacuated(dve, len(CHUNKS) - 1)
                evacuated(dve, len(CHUNKS) - 2)
                for p in range(3):
                    for m in range(MT):
                        cols = slice(p * PIECE, (p + 1) * PIECE)
                        ins = dve.scalar_tensor_tensor(out=x_sb[:, m, cols], in0=y[:, m, cols], scalar=rstd[:, m:m + 1],
                                                       in1=x_sb[:, m, cols], op0=ALU.mult, op1=ALU.add)
                    ins.then_inc(x_new, 1)
                for b in range(2):
                    dve.wait_ge(first_hi_ready, b + 1)
                    split_x_lo(dve, b, xT_ready)

            @block.tensor
            def _(pe):
                def mm(out, a, b, start=True, stop=True):
                    return pe.matmul(out, a, b, start=start, stop=stop)

                def stream(s, between):
                    c, q = STEPS[s]
                    kind, i, k = CHUNKS[c]
                    slot = s % 2
                    if q == 0 and c >= 2:
                        pe.wait_ge(acc_free[c % 2], c // 2)
                    if c == 0 and q:
                        pe.wait_ge(xT_ready, 2 * q)
                    if kind[:2] == "z_" and i == 0 and q == 0:
                        pe.wait_ge(branch_lo, {"z_a": 1, "z_b": 3, "z_c": 7}[kind])
                    if kind == "out" and i == 0:
                        pe.wait_ge(branch_lo, 8 + q)
                    if s:
                        pe.wait_ge(hi_ready, s)
                    for t in range(QK):
                        w = w_hi[:, slot, t * CW:(t + 1) * CW]
                        for n, part in enumerate(lhs(c, QK * q + t)):
                            for m in range(MT):
                                mm(acc[c % 2][:, m * CW:(m + 1) * CW], part[:, m * P:(m + 1) * P], w,
                                   start=(q == 0 and t == 0 and n == 0), stop=False)
                    between()
                    if s:
                        pe.wait_ge(lo_dve, s)
                        pe.wait_ge(lo_pool, s)
                    for t in range(QK):
                        w = w_lo[:, slot, t * CW:(t + 1) * CW]
                        part = lhs(c, QK * q + t)[0]
                        for m in range(MT):
                            ins = mm(acc[c % 2][:, m * CW:(m + 1) * CW], part[:, m * P:(m + 1) * P], w, start=False,
                                     stop=(q == k // QK - 1 and t == QK - 1))
                    ins.then_inc(pe_step, 1)

                def turn(c):
                    n = 2 if CHUNKS[c][0] == "rope_kv" else 4
                    if c in ROPED:
                        pe.wait_ge(roped, ROPED.index(c) + 1)
                    else:
                        pe.wait_ge(staged, TURNED.index(c) + 1)
                    for h in range(n):
                        for m in range(MT):
                            ins = pe.transpose(acc[c % 2][:, h * T + m * P:h * T + (m + 1) * P],
                                               stage[:, m, h * HD:(h + 1) * HD], ident)
                    ins.then_inc(turned, 1)

                def level_grams(s):
                    for u in range(4):
                        l = s - 1 - REC[u] - FIRST_LEVEL
                        if not -1 <= l < LEVELS:
                            continue
                        q = rec_views(u)[0]
                        n = (LEVELS + 1) * u + l + 1
                        pe.wait_ge(mixed, n + 1)
                        if n >= 2:
                            pe.wait_ge(kept, n - 1)
                        if n == 0:
                            pe.wait_ge(branch_lo, 3)
                        dst = side[0][:, n % 2 * 512:n % 2 * 512 + 512]
                        for b in range(4):
                            h, st = divmod(b, 2)
                            tt = 1 - st if l == LEVELS - 1 else st
                            qq = q if l < 0 else EQ[:, 3]
                            ins = mm(dst[:, b * P:(b + 1) * P], EQ[:, 2, h * T + st * P:h * T + (st + 1) * P],
                                     qq[:, h * T + tt * P:h * T + (tt + 1) * P])
                        ins.then_inc(grams, 1)

                for s in range(NSTEPS):
                    stream(s, lambda: level_grams(s))
                    c = ENDS.get(s - 1)
                    if c is not None and c in TURNED and c not in ROPED:
                        turn(c)
                    c = ENDS.get(s - 2)
                    if c is not None and c in ROPED:
                        turn(c)
                    for u, s0 in enumerate(UNITS):
                        q, k, m = unit(u)
                        if s == s0:
                            if u == 0:
                                for g in range(2 * NG):
                                    evacuated(pe, 1 + g)
                            elif u == A_UNITS:
                                for g in range(3):
                                    evacuated(pe, CHUNKS.index(("rope_qb", 0, KT)) + g)
                                pe.wait_ge(branch_lo, 1)
                            if u:
                                pe.wait_ge(masked, u)
                            for i in range(len(q)):
                                ins = mm(side[0][:, i * T:(i + 1) * T], q[i], k[i])
                            ins.then_inc(scored, 1)
                        if s == s0 + 2:
                            pe.wait_ge(probs, u + 1)
                            if u:
                                pe.wait_ge(normed, u)
                            for i in range(len(q)):
                                for t in range(MT):
                                    at = (257 if u >= A_UNITS else T) * i + t * P
                                    ins = pe.transpose(side[1][:, (2 * i + t) * P:(2 * i + t + 1) * P], scores[:, at:at + P],
                                                       ident)
                            ins.then_inc(probs_turned, 1)
                        if s == s0 + 3:
                            pe.wait_ge(probs_copied, u + 1)
                            if u == 0:
                                for g in range(NG):
                                    evacuated(pe, 1 + 2 * NG + g)
                            for i in range(len(q)):
                                for t in range(MT):
                                    w = probsT[:, (2 * i + t) * P:(2 * i + t + 1) * P]
                                    if u < A_UNITS:
                                        h = u // MT
                                        ins = mm(side[1][:, 0:P], w, va[:, i, t, h * HD:(h + 1) * HD],
                                                 start=(i == 0 and t == 0), stop=(i == NG - 1 and t == MT - 1))
                                    else:
                                        kv = (u - A_UNITS) // MT
                                        ins = mm(side[1][:, i * P:(i + 1) * P], w, vb[:, t, kv * HD:(kv + 1) * HD],
                                                 start=(t == 0), stop=(t == MT - 1))
                            ins.then_inc(attended, 1)
                    for u in range(4):
                        d = s - REC[u]
                        _, _, v, _, _, j = rec_views(u)
                        nine = (LEVELS + 1) * u
                        if d == FIRST_LEVEL + 8:
                            pe.wait_ge(kept, nine + LEVELS + 1)
                            evacuated(pe, CHUNKS.index(("c_v", u // 2, KT)))
                            if u:
                                pe.wait_ge(rec_y, u)
                            for h in range(2):
                                for tt in range(MT):
                                    i = h * MT + tt
                                    o = side[1][:, i * P:(i + 1) * P]
                                    mm(o, S_diag[:, i], v[:, tt, (j + h) * HD:(j + h + 1) * HD], stop=False)
                                    ins = mm(o, S_off[:, h * MT + 1 - tt], v[:, 1 - tt, (j + h) * HD:(j + h + 1) * HD],
                                             start=False)
                            ins.then_inc(rec_out, 1)
                    if s in TURN_AT:
                        n = TURN_AT[s]
                        _, src, first_, blocks, _, _, _, ps = turns[n]
                        if n == 0:
                            pe.wait_ge(normed, A_UNITS)
                        elif n <= 2:
                            pe.wait_ge(normed, A_UNITS + B_UNITS)
                        elif n <= 6:
                            pe.wait_ge(rec_y, n - 2)
                            pe.wait_ge(normed, A_UNITS + B_UNITS)
                        else:
                            pe.wait_ge(summed, 4 + n - 6)
                            pe.wait_ge(kept, 4 * (LEVELS + 1))
                        if n:
                            pe.wait_ge(branch_lo, n)
                        for i in range(blocks):
                            for m in range(MT):
                                ins = pe.transpose(ps[:, i * T + m * P:i * T + (m + 1) * P],
                                                   src[:, m, (first_ + i) * P:(first_ + i + 1) * P], ident)
                        ins.then_inc(branch_turned, 1)
                for p in range(4):
                    if p < 3:
                        pe.wait_ge(x_new, p + 1)
                    else:
                        pe.wait_ge(x_new_pool, 1)
                    turn_x(pe, p)

        with nc.Fori(0, DEPTH) as layer:
            with nc.Block() as block:
                layer_body(layer, block)
            counts_from_zero()

        with nc.Block() as block:
            @block.sync
            def _(sp):
                sp.wait_ge(x_stored, 64 * (DEPTH + 1))


def constants():
    pos = np.arange(T, dtype=np.float32)
    freq = np.float32(THETA) ** (-np.arange(0, ROT, 2, dtype=np.float32) / np.float32(ROT))
    ang = (pos[:, None] * freq[None, :]).astype(np.float32)
    cos, sin = np.cos(ang), np.sin(ang)
    by_tile = lambda v: v.reshape(MT, P, ROT).transpose(1, 0, 2).reshape(P, MT * ROT)
    const = np.concatenate([np.eye(P, dtype=np.float32), by_tile(np.concatenate([cos, cos], 1)),
                            by_tile(np.concatenate([-sin, sin], 1))], 1).astype(np.float32)
    i = np.arange(T)
    rel = np.abs(i[:, None] - i[None, :])
    allowed = [(rel % dil == 0) & (rel // dil <= window // (2 * dil)) for window, dil in GROUPS] + [rel <= BWIN]
    masks = np.stack([np.where(a, 0.0, NEG) for a in allowed], 1).astype(np.float32)
    masks = masks.reshape(MT, P, (NG + 1) * T).transpose(1, 0, 2).reshape(P, -1)
    p = np.arange(P)
    levels = [((p[:, None] >> (l + 1)) == (p[None, :] >> (l + 1))) & ((p[:, None] >> l) != (p[None, :] >> l))
              for l in range(LEVELS - 1)]
    lmasks = np.stack(levels, 1).astype(np.float32).reshape(P, -1)
    return const, np.ascontiguousarray(masks), np.ascontiguousarray(lmasks)


def tiles(w):
    k, n = w.shape
    return w.reshape(k // (P * QK), QK, P, n // CW, CW).transpose(3, 0, 2, 1, 4)


W_IN_ORDER = [9, 0, 1, 2, 3, 4, 5, 6, 7, 8, 13, 14, 10, 11, 12, 15, 17, 19, 21, 23, 16, 18, 20, 22, 24]


def stream_of(w_in, w_a, w_b, w_c, w_out):
    t = tiles(w_in)
    parts = [t[c] for c in W_IN_ORDER]
    for b, w in enumerate((w_a, w_b, w_c)):
        z = tiles(w)
        for j in range(4):
            parts += [t[25 + 4 * b + j], z[j]]
    parts += list(tiles(w_out))
    return np.concatenate(parts, 0).reshape(NSTEPS, P, TILE)


def kernel(x, pre_norm, post_norm, w_in, sink_logits, hgrn_lower_bounds, hgrn_norm, w_branch_a, w_branch_b,
           w_branch_c, w_out):
    import concourse.bacc as bacc
    from concourse.bass_utils import run_bass_kernel_spmd

    x, pre_norm, post_norm, w_in, sink_logits, hgrn_lower_bounds, hgrn_norm, w_branch_a, w_branch_b, w_branch_c, w_out = (
        np.asarray(a) for a in (x, pre_norm, post_norm, w_in, sink_logits, hgrn_lower_bounds, hgrn_norm, w_branch_a,
                                w_branch_b, w_branch_c, w_out))
    const, masks, lmasks = constants()
    by_channel = lambda v: v.reshape(-1, P).T
    sel = [np.full((P, 1), float(layer > 0), np.float32) for layer in range(DEPTH)]
    par = np.stack([np.concatenate(
        [by_channel(pre_norm[n]), by_channel(hgrn_norm[n]), np.broadcast_to(sink_logits[n], (P, BQ)),
         by_channel(hgrn_lower_bounds.reshape(-1)), sel[n]], 1) for n in [*range(DEPTH), DEPTH - 1]])
    weights = [stream_of(w_in[n], w_branch_a[n], w_branch_b[n], w_branch_c[n], w_out[n]) for n in range(DEPTH)]
    weights = np.concatenate([*weights, weights[0][:3]])
    arrays = {"w_stream": weights, "x_in": x, "const_in": const, "masks_in": masks, "lmasks_in": lmasks,
              "params_in": np.ascontiguousarray(par), "post_in": post_norm}
    nc = bacc.Bacc("TRN2", target_bir_lowering=False, num_devices=1)
    aps = [nc.dram_tensor(n, a.shape, mybir.dt.from_np(a.dtype), kind="ExternalInput").ap() for n, a in arrays.items()]
    out = nc.dram_tensor("x_out", x.shape, F32, kind="ExternalOutput").ap()
    build(nc, *aps, out)
    r = run_bass_kernel_spmd(nc, [arrays], core_ids=[0])
    return r.results[0]["x_out"]
```

```python
from contextlib import ExitStack

import numpy as np

import concourse.bass as bass
from concourse import mybir

ALU = mybir.AluOpType
ACT = mybir.ActivationFunctionType
AX = mybir.AxisListType
F32 = mybir.dt.float32
F32R = mybir.dt.float32r
BF16 = mybir.dt.bfloat16
U8 = mybir.dt.uint8

P = 128
D = 2048
T = 256
MT = T // P
DEPTH = 2
KT = D // P
CW = 512
QK = 4
TILE = QK * CW
EPS = 1e-6
HD = 128
ROT = HD // 4
HALF = ROT // 2
THETA = 500000.0
SCALE = float(HD) ** -0.5
NEG = -1e30
GROUPS = ((128, 1), (512, 4), (2048, 16))
NG = len(GROUPS)
assert GROUPS[0][1] == 1 and all(dil % MT == 0 for _, dil in GROUPS[1:])
A_COLS = T + (NG - 1) * P
MASK_COLS = A_COLS + T
SLOTS = D // 512
BQ = D // 256
BKV = BQ // 4
BWIN = 128
CH = D // 256
LEVELS = 8
TINY = 1e-18
LN_TINY = float(-np.log(TINY))

CHUNKS = [("rope_qa", g, KT) for g in range(NG)] + [("rope_ka", g, KT) for g in range(NG)]
CHUNKS += [("gate_a", 0, KT)] + [("v_a", g, KT) for g in range(NG)]
CHUNKS += [("gate_b", 0, KT), ("gate_b", 1, KT), ("rope_qb", 0, KT), ("rope_qb", 1, KT), ("rope_kv", 0, KT)]
for _g in range(2):
    CHUNKS += [(k, _g, KT) for k in ("c_q", "c_zf", "c_zb", "c_v", "gate_c")]
for _b, _k in (("a", SLOTS), ("b", BQ), ("c", CH)):
    for _j in range(4):
        CHUNKS += [("merge_" + _b, _j, KT), ("z_" + _b, _j, _k)]
CHUNKS += [("out", j, KT) for j in range(4)]

STEP_OF = []
STEPS = []
for _c, (_kind, _i, _k) in enumerate(CHUNKS):
    STEP_OF.append(len(STEPS))
    STEPS += [(_c, q) for q in range(_k // QK)]
NSTEPS = len(STEPS)
ENDS = {}
for _c, (_kind, _i, _k) in enumerate(CHUNKS):
    ENDS[STEP_OF[_c] + _k // QK - 1] = _c


def end_of(kind, i):
    c = [n for n, x in enumerate(CHUNKS) if x[:2] == (kind, i)][0]
    return STEP_OF[c] + CHUNKS[c][2] // QK - 1


TURNED = [c for c, x in enumerate(CHUNKS) if x[0].startswith("rope") or x[0] in ("c_q", "c_zf", "c_zb")]
ROPED = [c for c in TURNED if CHUNKS[c][0].startswith("rope")]
MERGES = [c for c, x in enumerate(CHUNKS) if x[0].startswith("merge")]

A_UNITS = SLOTS * MT
B_UNITS = BKV * MT
UNITS = [end_of("v_a", NG - 1) + 2 + 2 * u for u in range(A_UNITS)]
UNITS += [end_of("rope_kv", 0) + 4 + 2 * u for u in range(B_UNITS)]
TURN_A = UNITS[A_UNITS - 1] + 5
TURN_B = [UNITS[-1] + 6, UNITS[-1] + 8]
REC = [TURN_B[1] + 2 + 15 * u for u in range(4)]
FIRST_LEVEL = 7
Z_A_END = end_of("z_a", 3)
TURN_C = [Z_A_END + 1, Z_A_END + 3, REC[3] + 5, REC[3] + FIRST_LEVEL + 11]
LANDING = 4
assert NSTEPS % LANDING == 0
SP_EXTRA = TURN_C[3] + 3 + LANDING
assert TURN_C[3] + 2 < end_of("z_c", 0) and SP_EXTRA + 6 < STEP_OF[CHUNKS.index(("out", 0, KT))]
APART_AT = 4
MASKS_AT = 7

SILUS = [c for c, x in enumerate(CHUNKS) if x[0].startswith("gate") or x[0] == "c_q"]
SPLIT = 1280
PIECE = D // 4
PARAMS = KT + CH + BQ + DEPTH * CH + 1


def build(nc, W, X, CONST, MASKS, LMASKS, PAR, POST, OUT):
    out_v = OUT.rearrange("b (m p) d -> p (b m) d", p=P)
    x_v = X.rearrange("b (m p) d -> p (b m) d", p=P)
    with ExitStack() as ctx:
        def sb(name, shape, dt=F32):
            return ctx.enter_context(nc.sbuf_tensor(name, shape, dt))

        def sem(name):
            return ctx.enter_context(nc.semaphore(name))

        K1 = 1024
        place = (nc.sbuf_base + 31) // 32 * 32
        sb("arena_fence", [P, 76 * K1 // 4 + 8])
        arena = nc.alloc_sbuf_tensor_at("arena", [P, 76 * K1 // 4], F32, offset=place)

        w_place = (nc.sbuf_base + 31) // 32 * 32
        sb("weights_fence", [P, LANDING * TILE + 8])
        raw = nc.alloc_sbuf_tensor_at("raw", [P, LANDING, TILE], F32, offset=w_place)
        w_lo = nc.alloc_sbuf_tensor_at("w_lo", [P, LANDING, TILE], F32R, offset=w_place)
        w_hi = sb("w_hi", [P, 2, TILE], F32R)
        xT_hi = sb("xT_hi", [P, KT, T], F32R)
        xT_lo = sb("xT_lo", [P, KT, T], F32R)
        aT_hi = sb("aT_hi", [P, 4, T], F32R)
        aT_lo = sb("aT_lo", [P, 4, T], F32R)
        bT_hi = sb("bT_hi", [P, BQ, T], F32R)
        bT_lo = sb("bT_lo", [P, BQ, T], F32R)
        stage = sb("stage", [P, MT, CW])
        wide = sb("wide", [P, 1028 + 1024])
        scores = wide[:, 0:1028]
        probsT = wide[:, 1028:2052]
        ropes = sb("ropes", [P, 2, MT * 4 * ROT])
        const = sb("const", [P, P + MT * ROT * 2])
        masks = sb("masks", [P, MT, MASK_COLS], BF16)
        lmasks = sb("lmasks", [P, LEVELS - 1, P], U8)
        par = sb("par", [P, PARAMS])
        lbs = sb("lbs", [P, 8, CH])
        small = sb("small", [P, 64])
        small2 = sb("small2", [P, 64])
        half_neg = sb("half_neg", [P, 1])
        def piece(at, shape, dt=F32):
            n = int(np.prod(shape))
            v = arena[:, at * K1 // 4: at * K1 // 4 + n]
            if len(shape) == 2:
                return v.rearrange("p (a b) -> p a b", b=shape[1])
            if len(shape) == 3:
                return v.rearrange("p (a b c) -> p a b c", b=shape[1], c=shape[2])
            return v

        qaT = piece(0, [NG * SLOTS, T])
        kaT = piece(12, [NG * SLOTS, T])
        va = piece(24, [NG, MT, CW])
        gate_a = piece(36, [MT, CW])
        qbT = piece(40, [BQ, T])
        kbT = piece(48, [BKV, T])
        vb = piece(50, [MT, BKV * HD])
        gate_b = piece(52, [2, MT, CW])
        cq = [piece(20 * g, [4, T]) for g in range(2)]
        cz = [[piece(20 * g + 4, [4, T]), piece(20 * g + 8, [4, T])] for g in range(2)]
        cv = [piece(20 * g + 12, [MT, CW]) for g in range(2)]
        gate_c = [piece(20 * g + 16, [MT, CW]) for g in range(2)]
        PI = piece(40, [2, 512])
        RX = piece(44, [2, 512])
        EQ = piece(48, [4, 512])
        S_diag = piece(56, [4, P])
        S_off = piece(58, [4, P])
        y_turned = piece(56, [4, T])
        ab_turned = piece(60, [4, T])
        q_tanh = piece(64, [4, T])
        c_turned = probsT[:, 0:2 * T].rearrange("p (h t) -> p h t", t=T)
        y = piece(60, [MT, D])
        x_sb = piece(40, [MT, D])
        ident = const[:, 0:P]
        cosT = const[:, P:P + MT * ROT].rearrange("p (m r) -> p m r", m=MT)
        sinT = const[:, P + MT * ROT:P + 2 * MT * ROT].rearrange("p (m r) -> p m r", m=MT)
        pre_gain = par[:, 0:KT]
        hg_gain = par[:, KT:KT + CH]
        sink = par[:, KT + CH:KT + CH + BQ]
        lb_raw = par[:, KT + CH + BQ:KT + CH + BQ + DEPTH * CH].rearrange("p (l h) -> p l h", l=DEPTH)
        lb_sel = par[:, PARAMS - 1:PARAMS]
        lb, one_lb, lb_tiny = lbs[:, 0], lbs[:, 1], lbs[:, 2]
        x_sumsq = small[:, 20:22]
        x_rstd = small[:, 22:24]
        half_rstd = small[:, 24:26]
        apart_pair = small[:, 28:32].rearrange("p (k m) -> p k m", m=MT)
        rstd_apart, half_rstd_apart = apart_pair[:, 0], apart_pair[:, 1]
        sumsq = small[:, 0:2]
        rstd = small[:, 2:4]
        out_sq = small[:, 4:12]
        rec_sq = small[:, 12:16]
        rec_rstd = small[:, 16:20]
        smax = small2[:, 0:8].rearrange("p (b i) -> p b i", b=2)
        nmax = small2[:, 8:16].rearrange("p (b i) -> p b i", b=2)
        dens = small2[:, 16:24].rearrange("p (b i) -> p b i", b=2)
        rden = small2[:, 24:32].rearrange("p (b i) -> p b i", b=2)
        post_gain = wide[:, 0:D]

        yT_hi = nc.alloc_sbuf_tensor_at("yT_hi", [P, KT, T], F32R, offset=place + 8 * K1)
        yT_lo = nc.alloc_sbuf_tensor_at("yT_lo", [P, KT, T], F32R, offset=place + 24 * K1)
        cT_hi = nc.alloc_sbuf_tensor_at("cT_hi", [P, 4, T], F32R, offset=place)
        cT_lo = nc.alloc_sbuf_tensor_at("cT_lo", [P, 4, T], F32R, offset=place + 4 * K1)

        acc = [ctx.enter_context(nc.psum_tensor(f"acc{i}", [P, MT * CW], F32)) for i in range(2)]
        side = [ctx.enter_context(nc.psum_tensor(f"side{i}", [P, MT * CW], F32)) for i in range(2)]
        accv = [a[:, :].rearrange("p (m c) -> p m c", m=MT) for a in acc]

        x_stored = sem("x_stored")
        const_landed = sem("const_landed")
        x_in = [sem(f"x_in{p}") for p in range(4)]
        first_landed = [sem(f"first_landed{i}") for i in range(LANDING)]
        names = """w_landed0 w_landed1 w_landed2 w_landed3 acc_free0 acc_free1 par_landed masks_landed x_landed hi_ready lo_dve lo_pool
            pe_step dve_chain pool_chain x_squared x_rstd_ready sorter_ready rstd_sorted apart_ready x_turned xT_hi_ready xT_ready
            first_hi_ready staged roped turned tanhed scored masked probs probs_turned probs_copied attended
            normed branch_turned branch_hi branch_lo lb_ready rec_prep rec_exp rx_cleared logs_ready mixed grams
            decays scanned kept rec_out rec_squared rec_rstd_ready rec_y gated summed out_squared out_summed
            out_rstd y_scaled x_new x_new_pool""".split()
        (w_landed0, w_landed1, w_landed2, w_landed3, acc_free0, acc_free1, par_landed, masks_landed, x_landed, hi_ready, lo_dve, lo_pool,
         pe_step, dve_chain, pool_chain, x_squared, x_rstd_ready, sorter_ready, rstd_sorted, apart_ready, x_turned, xT_hi_ready, xT_ready,
         first_hi_ready, staged, roped, turned, tanhed, scored, masked, probs, probs_turned, probs_copied, attended,
         normed, branch_turned, branch_hi, branch_lo, lb_ready, rec_prep, rec_exp, rx_cleared, logs_ready, mixed,
         grams, decays, scanned, kept, rec_out, rec_squared, rec_rstd_ready, rec_y, gated, summed, out_squared,
         out_summed, out_rstd, y_scaled, x_new, x_new_pool) = per_layer = [sem(n) for n in names]
        w_landed = [w_landed0, w_landed1, w_landed2, w_landed3]
        acc_free = [acc_free0, acc_free1]

        flat = lambda v: v.rearrange("p h t -> p (h t)")
        turns = [(TURN_A, gate_a, 4, aT_hi[:, :, :], aT_lo[:, :, :], None, flat(ab_turned))]
        for r in range(2):
            turns.append((TURN_B[r], gate_b[:, r], 4, bT_hi[:, 4 * r:4 * r + 4], bT_lo[:, 4 * r:4 * r + 4],
                          None, flat(ab_turned)))
        for u in range(4):
            g, j = u // 2, 2 * (u % 2)
            hi, lo = (aT_hi, aT_lo) if g == 0 else (cT_hi, cT_lo)
            turns.append((TURN_C[u], gate_c[g][:, :, j * HD:(j + 2) * HD], 2, hi[:, j:j + 2, :], lo[:, j:j + 2, :],
                          hg_gain[:, 4 * g + j:4 * g + j + 2], flat(c_turned)))
        for j in range(4):
            turns.append((end_of("z_c", j) + 2, y[:, :, j * CW:(j + 1) * CW], 4, yT_hi[:, 4 * j:4 * j + 4, :],
                          yT_lo[:, 4 * j:4 * j + 4, :], None,
                          side[1][:, :] if j == 3 else flat(y_turned)))
        TURN_AT = {t[0]: n for n, t in enumerate(turns)}
        BY_BLOCKS = range(len(turns) - 1)

        def split_at(s):
            n = TURN_AT.get(s - 1)
            m = TURN_AT.get(s - 2)
            return m if m in BY_BLOCKS else n if n not in BY_BLOCKS else None

        def lhs(c, k):
            kind = CHUNKS[c][0]
            if kind == "out":
                return yT_hi[:, k, :], yT_lo[:, k, :]
            if kind == "z_a" or (kind == "z_c" and k < 4):
                return aT_hi[:, k, :], aT_lo[:, k, :]
            if kind == "z_b":
                return bT_hi[:, k, :], bT_lo[:, k, :]
            if kind == "z_c":
                return cT_hi[:, k - 4, :], cT_lo[:, k - 4, :]
            return xT_hi[:, k, :], xT_lo[:, k, :]

        def halves(v, level):
            w = v.rearrange("p (n two l) -> p n two l", two=2, l=1 << level)
            return w[:, :, 0, :], w[:, :, 1, :]

        def apart(v):
            return v.rearrange("p (t m) -> p m t", m=MT)

        def unit(u):
            if u < A_UNITS:
                h, m = divmod(u, MT)
                q = [apart(qaT[:, g * SLOTS + h, :])[:, m] for g in range(NG)]
                k = [apart(kaT[:, g * SLOTS + h, :]) for g in range(NG)]
                return q, [k[0]] + [v[:, m] for v in k[1:]], m
            kv, m = divmod(u - A_UNITS, MT)
            q = [qbT[:, 4 * kv + i, m * P:(m + 1) * P] for i in range(4)]
            return q, [kbT[:, kv, :]] * 4, m

        def key_tiles(u):
            if u < A_UNITS:
                return [(t * P, 0, t) for t in range(MT)] + [(T + (g - 1) * P, g, u % MT) for g in range(1, NG)]
            return [(257 * i + t * P, i, t) for i in range(4) for t in range(MT)]

        def rec_views(u):
            g, j = u // 2, 2 * (u % 2)
            flat = lambda v: v[:, j:j + 2, :].rearrange("p h t -> p (h t)")
            return flat(cq[g]), [flat(z) for z in cz[g]], cv[g], gate_c[g], 4 * g + j, j

        def columns(v, p):
            return v[:, :, p * PIECE:(p + 1) * PIECE]

        def x_blocks(b):
            return (acc[0], acc[1], side[0], side[1])[b // 2][:, (b % 2) * 512:(b % 2) * 512 + 512]

        def turn_x(pe, p):
            for b in (2 * p, 2 * p + 1):
                for m in range(MT):
                    for i in range(2):
                        k = 2 * b + i
                        ins = pe.transpose(x_blocks(b)[:, i * T + m * P:i * T + (m + 1) * P], x_sb[:, m, k * P:(k + 1) * P],
                                           ident)
            ins.then_inc(x_turned, 1)

        def split_x_hi(act, b, done):
            for i in range(2):
                k = 2 * b + i
                ins = act.activation(xT_hi[:, k, :], x_blocks(b)[:, i * T:(i + 1) * T], ACT.Copy, scale=pre_gain[:, k:k + 1])
            ins.then_inc(done, 1)

        def split_x_lo(dve, b, done):
            for i in range(2):
                k = 2 * b + i
                ins = dve.scalar_tensor_tensor(out=xT_lo[:, k, :], in0=x_blocks(b)[:, i * T:(i + 1) * T],
                                               scalar=pre_gain[:, k:k + 1], in1=xT_hi[:, k, :].bitcast(F32),
                                               op0=ALU.mult, op1=ALU.subtract)
            ins.then_inc(done, 1)

        def w_hi_of(act, s):
            return act.activation(w_hi[:, s % 2, :], raw[:, s % LANDING, :], ACT.Copy)

        def w_lo_of(eng, s, cols):
            return eng.tensor_tensor(w_lo[:, s % LANDING, cols], raw[:, s % LANDING, cols], w_hi[:, s % 2, cols].bitcast(F32),
                                     ALU.subtract)

        DVE_COLS, POOL_COLS = slice(0, SPLIT), slice(SPLIT, TILE)

        def counts_from_zero():
            numbers = [q.num for q in per_layer]
            assert numbers == list(range(numbers[0], numbers[0] + len(numbers)))
            nc.gpsimd.sem_clear(range(numbers[0], numbers[-1] + 1))
            nc.all_engine_barrier()

        with nc.Block() as block:
            @block.sync
            def _(sp):
                sp.dma_start(columns(x_sb, 0), columns(x_v, 0)).then_inc(x_in[0], 16)
                sp.dma_start(raw[:, 0, :], W[0]).then_inc(first_landed[0], 16)
                for p in range(1, 4):
                    sp.dma_start(columns(x_sb, p), columns(x_v, p)).then_inc(x_in[p], 16)
                for s in range(1, LANDING):
                    sp.dma_start(raw[:, s, :], W[s]).then_inc(first_landed[s], 16)
                for p in range(4):
                    sp.wait_ge(x_in[p], 16)
                    sp.dma_start(columns(out_v, p), columns(x_sb, p)).then_inc(x_stored, 16)

            @block.gpsimd
            def _(pool):
                pool.memset(half_neg[:, :], -0.5)
                pool.wait_ge(hi_ready, 1)
                w_lo_of(pool, 0, POOL_COLS)

            @block.scalar
            def _(act):
                act.dma_start(const[:, :], CONST).then_inc(const_landed, 16)
                act.dma_start(par[:, :], PAR[0]).then_inc(par_landed, 16)
                act.wait_ge(par_landed, 16)
                act.wait_ge(x_turned, 1)
                for b in range(2):
                    split_x_hi(act, b, first_hi_ready)
                act.wait_ge(first_landed[0], 16)
                w_hi_of(act, 0).then_inc(hi_ready, 1)

            @block.vector
            def _(dve):
                for b in range(2):
                    dve.wait_ge(first_hi_ready, b + 1)
                    split_x_lo(dve, b, xT_ready)
                dve.wait_ge(hi_ready, 1)
                w_lo_of(dve, 0, DVE_COLS)

            @block.tensor
            def _(pe):
                pe.wait_ge(const_landed, 16)
                for p in range(4):
                    pe.wait_ge(x_in[p], 16)
                    turn_x(pe, p)
        counts_from_zero()

        def evacuated(eng, c):
            if c in TURNED:
                eng.wait_ge(staged, TURNED.index(c) + 1)
            else:
                eng.wait_ge(acc_free[c % 2], len([x for x in range(c % 2, c + 1, 2) if x not in TURNED]))

        def layer_body(layer, block):
            @block.sync
            def _(sp):
                for s in range(LANDING, NSTEPS + LANDING):
                    sp.wait_ge(pe_step, s - LANDING + 1)
                    landed = w_landed[s % LANDING] if s < NSTEPS else first_landed[s - NSTEPS]
                    sp.dma_start(raw[:, s % LANDING, :], W[layer * NSTEPS + s]).then_inc(landed, 16)
                    if s == LANDING:
                        sp.dma_start(y[:, 0, 0:MT * MASK_COLS],
                                     MASKS).then_inc(masks_landed, 16)
                        sp.dma_start(y[:, 1, 0:(LEVELS - 1) * P], LMASKS).then_inc(masks_landed, 16)
                    p = s - SP_EXTRA
                    if 0 <= p < 4:
                        if p == 0:
                            sp.wait_ge(x_stored, 64 * (layer + 1))
                            sp.wait_ge(branch_lo, 7)
                        sp.dma_start(columns(x_sb, p), columns(out_v, p)).then_inc(x_landed, 16)
                    if p == 4:
                        sp.dma_start(post_gain, POST[layer].partition_broadcast(P)).then_inc(x_landed, 16)
                        sp.dma_start(par[:, :], PAR[layer + 1]).then_inc(par_landed, 16)
                for p in range(4):
                    if p == 0:
                        sp.wait_ge(x_landed, 80)
                    if p < 3:
                        sp.wait_ge(x_new, p + 1)
                    else:
                        sp.wait_ge(x_new_pool, 1)
                    sp.dma_start(columns(out_v, p), columns(x_sb, p)).then_inc(x_stored, 16)

            @block.gpsimd
            def _(pool):
                count = [0]

                def link(ins):
                    count[0] += 1
                    ins.then_inc(pool_chain, 1)
                    pool.wait_ge(pool_chain, count[0])

                def lo(s):
                    pool.wait_ge(hi_ready, s)
                    w_lo_of(pool, s, POOL_COLS).then_inc(lo_pool, 1)

                def power(dst, src, mean):
                    n = src.shape[1]
                    link(pool.tensor_scalar(dst, src, mean, EPS, ALU.mult, ALU.add))
                    return pool.tensor_tensor(dst, dst, half_neg[:, :].broadcast_to([P, n]), ALU.pow)

                for s in range(NSTEPS + 3):
                    if s < NSTEPS:
                        lo(s + 1)
                    if s == 3:
                        pool.wait_ge(x_squared, 2)
                        link(power(x_rstd, x_sumsq, 1.0 / D))
                        pool.tensor_scalar(half_rstd, x_rstd, 0.5, None, ALU.mult).then_inc(x_rstd_ready, 1)
                    for u in range(4):
                        if s == REC[u] + 6:
                            pool.wait_ge(rec_prep, 2 * u + 2)
                            pool.memset(RX, 0.0).then_inc(rx_cleared, 1)
                        l = s - REC[u] - FIRST_LEVEL
                        if 0 <= l < LEVELS - 1:
                            pool.wait_ge(decays, LEVELS * u + l + 1)
                            pf_lo, pf_up = halves(PI[:, 0], l)
                            rx_lo, _ = halves(RX[:, 0], l)
                            pb_lo, pb_up = halves(PI[:, 1], l)
                            _, rb_up = halves(RX[:, 1], l)
                            n, L = 512 >> (l + 1), 1 << l
                            last = lambda v: v[:, :, L - 1:L].broadcast_to([P, n, L])
                            head = lambda v: v[:, :, 0:1].broadcast_to([P, n, L])
                            pool.tensor_tensor(rx_lo, rx_lo, last(pf_up), ALU.add)
                            link(pool.tensor_tensor(rb_up, rb_up, head(pb_lo), ALU.add))
                            pool.tensor_tensor(pf_up, pf_up, last(pf_lo), ALU.add)
                            link(pool.tensor_tensor(pb_lo, pb_lo, head(pb_up), ALU.add))
                            pool.nop().then_inc(scanned, 1)
                        if s == REC[u] + FIRST_LEVEL + 9:
                            pool.wait_ge(rec_squared, u + 1)
                            link(power(rec_rstd, rec_sq, 1.0 / HD))
                            by_tile = lambda v: v.rearrange("p (h m) -> p h m", m=MT)
                            pool.tensor_tensor(by_tile(rec_rstd), by_tile(rec_rstd),
                                               x_rstd[:, None, :].broadcast_to([P, 2, MT]),
                                               ALU.mult).then_inc(rec_rstd_ready, 1)
                    for late, kind in ((2, "z_b"), (1, "z_c")):
                        c = ENDS.get(s - late)
                        if c is None or CHUNKS[c][0] != kind:
                            continue
                        n = [x for x in range(c + 1) if CHUNKS[x][0] in ("z_b", "z_c")]
                        j = CHUNKS[c][1]
                        pool.wait_ge(gated, len(n) + 4)
                        part = y[:, :, j * CW:(j + 1) * CW]
                        pool.tensor_tensor(part, part, stage[:, :, :], ALU.add).then_inc(summed, 1)
                pool.wait_ge(out_summed, 1)
                power(rstd, sumsq, 1.0 / D).then_inc(out_rstd, 1)
                pool.wait_ge(x_landed, 80)
                pool.wait_ge(y_scaled, 1)
                pool.tensor_tensor(columns(x_sb, 3), columns(x_sb, 3), columns(y, 3), ALU.add).then_inc(x_new_pool, 1)

            @block.scalar
            def _(act):
                def hi(s):
                    if s < LANDING:
                        act.wait_ge(first_landed[s], 16 * (layer + 1))
                    elif s == NSTEPS:
                        act.wait_ge(first_landed[0], 16 * (layer + 2))
                    else:
                        act.wait_ge(w_landed[s % LANDING], 16 * (s // LANDING))
                    if s >= 2:
                        act.wait_ge(pe_step, s - 1)
                    w_hi_of(act, s).then_inc(hi_ready, 1)

                def scaled(dst, src, func, scale, done=None):
                    for m in range(MT):
                        ins = act.activation(dst[:, m], src[:, m], func, scale=scale[:, m:m + 1])
                    if done is not None:
                        ins.then_inc(done, 1)

                for s in range(NSTEPS + 3):
                    if s < NSTEPS:
                        hi(s + 1)
                    if s == 0:
                        for b in range(2, KT // 2):
                            split_x_hi(act, b, xT_hi_ready)
                    if s in (1, 2):
                        if s == 2:
                            act.wait_ge(x_squared, 1)
                        act.activation(wide[:, 0:D], x_sb[:, s - 1, :], ACT.Square,
                                       accum_out=x_sumsq[:, s - 1:s]).then_inc(x_squared, 1)
                    if s == 3:
                        act.wait_ge(lb_ready, 1)
                        act.activation(lbs[:, 4:4 + DEPTH, :], lbs[:, 4:4 + DEPTH, :], ACT.Exp).then_inc(lb_ready, 1)
                        act.wait_ge(x_rstd_ready, 1)
                    c = ENDS.get(s - 1)
                    if c is not None:
                        kind, i, _ = CHUNKS[c]
                        act.wait_ge(pe_step, s)
                        if c in TURNED:
                            n = TURNED.index(c)
                            if n:
                                act.wait_ge(turned, n)
                            if kind == "rope_kv":
                                scaled(vb, accv[c % 2][:, :, T:2 * T], ACT.Copy, x_rstd)
                                scaled(stage[:, :, 0:T], accv[c % 2][:, :, 0:T], ACT.Copy, x_rstd, staged)
                            else:
                                scaled(stage, accv[c % 2], ACT.Copy, x_rstd, staged)
                        elif kind in ("v_a", "c_v"):
                            if kind == "c_v":
                                act.wait_ge(branch_turned, 1)
                            if kind == "v_a":
                                scaled(va[:, i], accv[c % 2], ACT.Copy, rstd_apart, acc_free[c % 2])
                            else:
                                scaled(cv[i], accv[c % 2], ACT.Copy, x_rstd, acc_free[c % 2])
                        elif kind.startswith("gate"):
                            dst = {"gate_a": lambda: gate_a, "gate_b": lambda: gate_b[:, i],
                                   "gate_c": lambda: gate_c[i]}[kind]()
                            if kind == "gate_b" and i == 0:
                                act.wait_ge(x_stored, 64 * (layer + 1))
                            if kind == "gate_c":
                                act.wait_ge(branch_turned, 1)
                            if kind == "gate_a":
                                act.wait_ge(apart_ready, 1)
                            scaled(dst, accv[c % 2], ACT.Tanh, half_rstd_apart if kind == "gate_a" else half_rstd, tanhed)
                        elif kind.startswith("merge"):
                            n = MERGES.index(c)
                            if n == 0:
                                act.wait_ge(turned, len(TURNED))
                            elif n <= 4:
                                act.wait_ge(gated, n)
                            else:
                                act.wait_ge(summed, n - 4)
                            scaled(stage, accv[c % 2], ACT.Tanh, half_rstd, acc_free[c % 2])
                        elif kind == "out":
                            act.wait_ge(summed, 8)
                            if i:
                                act.wait_ge(out_squared, 2 * i)
                            for m in range(MT):
                                act.activation(stage[:, m, :], accv[c % 2][:, m, :], ACT.Square,
                                               accum_out=out_sq[:, 4 * m + i:4 * m + i + 1]).then_inc(out_squared, 1)
                    c = ENDS.get(s - 5)
                    if c is not None and CHUNKS[c][0] == "c_q":
                        act.wait_ge(turned, TURNED.index(c) + 1)
                        act.activation(q_tanh, cq[CHUNKS[c][1]], ACT.Tanh, scale=0.5).then_inc(tanhed, 1)
                    for u, s0 in enumerate(UNITS):
                        if s == s0 + 2:
                            act.wait_ge(masked, u + 1)
                            b = u % 2
                            if u < A_UNITS:
                                act.activation(scores[:, 0:A_COLS], scores[:, 0:A_COLS], ACT.Exp, bias=nmax[:, b, 0:1],
                                               scale=SCALE, accum_out=dens[:, b, 0:1]).then_inc(probs, 1)
                            else:
                                for i in range(4):
                                    v = scores[:, 257 * i:257 * i + 257]
                                    ins = act.activation(v, v, ACT.Exp, bias=nmax[:, b, i:i + 1], scale=SCALE,
                                                         accum_out=dens[:, b, i:i + 1])
                                    if i == 3:
                                        ins.then_inc(probs, 1)
                        if s == s0 + 3:
                            act.wait_ge(probs_turned, u + 1)
                            if u:
                                act.wait_ge(attended, u)
                            n = P * len(key_tiles(u))
                            act.activation(probsT[:, 0:n], side[1][:, 0:n], ACT.Copy).then_inc(probs_copied, 1)
                    n = split_at(s)
                    if n is not None:
                        _, _, blocks, dst, _, gain, ps = turns[n]
                        act.wait_ge(branch_turned, n + 1)
                        src = ps.rearrange("p (i t) -> p i t", t=T)
                        if n == 0:
                            for m in range(MT):
                                ins = act.activation(dst.rearrange("p i (t m) -> p i m t", m=MT)[:, :, m],
                                                     src[:, :, m * P:(m + 1) * P], ACT.Copy, scale=0.5)
                            ins.then_inc(branch_hi, 1)
                        elif gain is None:
                            act.activation(dst, src, ACT.Copy, scale=0.5).then_inc(branch_hi, 1)
                        else:
                            for i in range(blocks):
                                ins = act.activation(dst[:, i], src[:, i], ACT.Copy, scale=gain[:, i:i + 1])
                            ins.then_inc(branch_hi, 1)
                    for u in range(4):
                        d = s - REC[u]
                        if d == 1:
                            act.wait_ge(rec_prep, 2 * u + 1)
                            act.activation(EQ, EQ, ACT.Exp).then_inc(rec_exp, 1)
                        if d == 6:
                            act.wait_ge(rec_prep, 2 * u + 2)
                            act.activation(EQ[:, 0:2], EQ[:, 0:2], ACT.Ln).then_inc(rec_exp, 1)
                        l = d - FIRST_LEVEL
                        if 0 <= l < LEVELS:
                            if l == 0:
                                act.wait_ge(logs_ready, u + 1)
                                act.wait_ge(rx_cleared, u + 1)
                            act.wait_ge(mixed, (LEVELS + 1) * u + l + 1)
                            if l:
                                act.wait_ge(scanned, (LEVELS - 1) * u + l)
                            ef_lo, ef_up = halves(EQ[:, 0], l)
                            eb_lo, eb_up = halves(EQ[:, 1], l)
                            act.activation(ef_up, halves(PI[:, 0], l)[1], ACT.Exp)
                            act.activation(ef_lo, halves(RX[:, 0], l)[0], ACT.Exp)
                            act.activation(eb_lo, halves(PI[:, 1], l)[0], ACT.Exp)
                            act.activation(eb_up, halves(RX[:, 1], l)[1], ACT.Exp).then_inc(decays, 1)
                        if d == FIRST_LEVEL + 9:
                            act.wait_ge(rec_out, u + 1)
                            for i in range(4):
                                ins = act.activation(wide[:, i * P:(i + 1) * P], side[1][:, i * P:(i + 1) * P], ACT.Square,
                                                     scale=0.5, accum_out=rec_sq[:, i:i + 1])
                            ins.then_inc(rec_squared, 1)
                act.wait_ge(out_rstd, 1)
                evacuated(act, len(CHUNKS) - 1)
                scaled(columns(y, 3), columns(y, 3), ACT.Copy, rstd, y_scaled)
                act.wait_ge(par_landed, 16)
                act.wait_ge(x_turned, 1)
                for b in range(2):
                    split_x_hi(act, b, first_hi_ready)

            @block.vector
            def _(dve):
                count = [0]

                def link(ins):
                    count[0] += 1
                    ins.then_inc(dve_chain, 1)
                    dve.wait_ge(dve_chain, count[0])

                def lo(s):
                    dve.wait_ge(hi_ready, s)
                    w_lo_of(dve, s, DVE_COLS).then_inc(lo_dve, 1)

                def lower_bounds():
                    link(dve.tensor_tensor(lbs[:, 3], lb_raw[:, 0], lb_raw[:, 1], ALU.max))
                    dve.tensor_tensor(lbs[:, 4], lb_raw[:, 0], lbs[:, 3], ALU.subtract)
                    dve.tensor_tensor(lbs[:, 5], lb_raw[:, 1], lbs[:, 3], ALU.subtract).then_inc(lb_ready, 1)
                    dve.tensor_scalar(hg_gain, hg_gain, 0.25, None, ALU.mult)
                    dve.tensor_scalar(sink, sink, 1.0 / SCALE, None, ALU.mult)
                    dve.wait_ge(lb_ready, 2)
                    link(dve.tensor_tensor(lbs[:, 6], lbs[:, 4], lbs[:, 5], ALU.add))
                    link(dve.reciprocal(lbs[:, 6], lbs[:, 6]))
                    link(dve.tensor_tensor(lbs[:, 6], lbs[:, 6], lbs[:, 5], ALU.mult))
                    link(dve.tensor_scalar(lb, lbs[:, 6], lb_sel, None, ALU.mult))
                    dve.tensor_scalar(one_lb, lb, -1.0, 1.0, ALU.mult, ALU.add)
                    link(dve.tensor_scalar(lb_tiny, lb, TINY, None, ALU.is_lt))

                def rope(c, n):
                    dve.wait_ge(staged, TURNED.index(c) + 1)
                    st = stage[:, :, 0:n * HD].rearrange("p m (h d) -> p m h d", d=HD)
                    ta = ropes[:, 0, 0:MT * n * ROT].rearrange("p (m h r) -> p m h r", m=MT, h=n)
                    tb = ropes[:, 1, 0:MT * n * ROT].rearrange("p (m h r) -> p m h r", m=MT, h=n)
                    wide_ = lambda v, w: v[:, :, None, :].broadcast_to([P, MT, n, w])
                    dve.tensor_tensor(ta, st[:, :, :, 0:ROT], wide_(cosT, ROT), ALU.mult)
                    dve.tensor_tensor(tb[:, :, :, 0:HALF], st[:, :, :, HALF:ROT], wide_(sinT[:, :, 0:HALF], HALF), ALU.mult)
                    link(dve.tensor_tensor(tb[:, :, :, HALF:ROT], st[:, :, :, 0:HALF], wide_(sinT[:, :, HALF:ROT], HALF),
                                           ALU.mult))
                    dve.tensor_tensor(st[:, :, :, 0:ROT], ta, tb, ALU.add).then_inc(roped, 1)

                def turn_blocks(dst, src, blocks):
                    for b in blocks:
                        ch, pos = slice(b // 4 * 32, b // 4 * 32 + 32), slice(b % 4 * 32, b % 4 * 32 + 32)
                        ins = dve.transpose(dst[ch].rearrange("p h (m t) -> p m h t", m=MT)[:, :, :, pos],
                                            src[pos].rearrange("p m (h d) -> p m h d", d=HD)[:, :, :, ch])
                    return ins

                def turn_chunk(c, blocks):
                    kind, i, _ = CHUNKS[c]
                    n = 2 if kind == "rope_kv" else 4
                    if kind in ("c_q", "c_zf", "c_zb"):
                        dve.wait_ge(branch_turned, 1)
                        dst = {"c_q": cq[i], "c_zf": cz[i][0], "c_zb": cz[i][1]}[kind]
                    else:
                        dst = {"rope_qa": qaT, "rope_ka": kaT, "rope_qb": qbT, "rope_kv": kbT}[kind][:, n * i:n * i + n]
                    ins = turn_blocks(dst, stage[:, :, 0:n * HD], blocks)
                    if 15 in blocks:
                        ins.then_inc(turned, 1)

                for s in range(NSTEPS + 3):
                    if s < NSTEPS:
                        lo(s + 1)
                    if s == 0:
                        for b in range(2, KT // 2):
                            dve.wait_ge(xT_hi_ready, b - 1)
                            split_x_lo(dve, b, xT_ready)
                    if s == 3:
                        lower_bounds()
                    if s == APART_AT - 1:
                        dve.wait_ge(x_squared, 2)
                        for m in range(MT):
                            ins = dve.tensor_copy(wide[:, m * P:(m + 1) * P].rearrange("p (i t) -> p i t", i=MT),
                                                  apart(ident)[:, m:m + 1].broadcast_to([P, MT, P // MT]))
                        ins.then_inc(sorter_ready, 1)
                    if s == APART_AT + 1:
                        dve.wait_ge(rstd_sorted, 1)
                        src = side[1][:, 0:8].rearrange("p (m k i) -> p k m i", m=MT, k=2)
                        for i in range(MT):
                            part = slice(i * P // MT, (i + 1) * P // MT)
                            ins = dve.tensor_copy(apart_pair[part], src[part, :, :, i])
                        ins.then_inc(apart_ready, 1)
                    if s == MASKS_AT:
                        dve.wait_ge(masks_landed, 32)
                        dve.tensor_copy(masks[:, :, :].rearrange("p m c -> p (m c)"),
                                        y[:, 0, 0:MT * MASK_COLS])
                    if s == MASKS_AT + 1:
                        dve.tensor_copy(lmasks[:, :, :].rearrange("p l c -> p (l c)"), y[:, 1, 0:(LEVELS - 1) * P])
                    for u in range(4):
                        d = s - REC[u]
                        q, z, _, gate, head, j = rec_views(u)
                        nine = (LEVELS + 1) * u
                        if d == 0:
                            if u == 0:
                                dve.wait_ge(branch_turned, 3)
                            else:
                                dve.wait_ge(grams, nine)
                            dve.wait_ge(turned, TURNED.index(CHUNKS.index(("c_zb", u // 2, KT))) + 1)
                            for x in range(2):
                                dve.tensor_scalar(EQ[:, x], z[x], 0.0, None, ALU.min)
                                dve.tensor_scalar(EQ[:, 2 + x], z[x], -1.0, 0.0, ALU.mult, ALU.min)
                                ins = dve.tensor_scalar(PI[:, x], z[x], LN_TINY, 0.0, ALU.add, ALU.min)
                            ins.then_inc(rec_prep, 1)
                        if d == 2:
                            dve.wait_ge(rec_exp, 2 * u + 1)
                            link(dve.tensor_tensor(RX, EQ[:, 0:2], EQ[:, 2:4], ALU.add))
                            dve.reciprocal(RX[:, 0], RX[:, 0])
                        if d == 3:
                            dve.reciprocal(RX[:, 1], RX[:, 1])
                            for x in range(2):
                                for h in range(2):
                                    cols = slice(h * T, (h + 1) * T)
                                    ins = dve.scalar_tensor_tensor(
                                        out=EQ[:, x, cols], in0=EQ[:, 2 + x, cols], scalar=lb[:, head + h:head + h + 1],
                                        in1=EQ[:, x, cols], op0=ALU.mult, op1=ALU.add)
                            link(ins)
                        if d == 4:
                            link(dve.tensor_tensor(EQ[:, 0:2], EQ[:, 0:2], RX, ALU.mult))
                            for x in range(2):
                                for h in range(2):
                                    cols = slice(h * T, (h + 1) * T)
                                    ins = dve.scalar_tensor_tensor(
                                        out=z[x][:, cols], in0=EQ[:, 2 + x, cols], scalar=one_lb[:, head + h:head + h + 1],
                                        in1=RX[:, x, cols], op0=ALU.mult, op1=ALU.mult)
                            link(ins)
                            dve.tensor_scalar(EQ[:, 0:2], EQ[:, 0:2], TINY, None, ALU.max).then_inc(rec_prep, 1)
                            dve.tensor_tensor(EQ[:, 2], z[0], z[1], ALU.add).then_inc(mixed, 1)
                        if d == 6:
                            dve.wait_ge(rec_exp, 2 * u + 2)
                            for x in range(2):
                                for h in range(2):
                                    cols = slice(h * T, (h + 1) * T)
                                    ins = dve.scalar_tensor_tensor(
                                        out=PI[:, x, cols], in0=PI[:, x, cols], scalar=lb_tiny[:, head + h:head + h + 1],
                                        in1=EQ[:, x, cols], op0=ALU.mult, op1=ALU.add)
                            ins.then_inc(logs_ready, 1)
                        l = d - FIRST_LEVEL
                        if 0 <= l < LEVELS:
                            dve.wait_ge(grams, nine + l + 1)
                            src = side[0][:, (nine + l) % 2 * 512:(nine + l) % 2 * 512 + 512].rearrange(
                                "p (b t) -> p b t", t=P)
                            if l == 0:
                                if u:
                                    dve.wait_ge(rec_out, u)
                                ins = dve.tensor_copy(S_diag, src)
                            else:
                                dve.wait_ge(kept, nine + l)
                                ins = dve.copy_predicated(S_diag, lmasks[:, l - 1:l, :].broadcast_to([P, 4, P]), src)
                            ins.then_inc(kept, 1)
                            dve.wait_ge(decays, LEVELS * u + l + 1)
                            (ef_lo, ef_up), (eb_lo, eb_up) = halves(EQ[:, 0], l), halves(EQ[:, 1], l)
                            (k_lo, k_up), (q_lo, q_up) = halves(EQ[:, 2], l), halves(EQ[:, 3], l)
                            dve.tensor_tensor(k_lo, halves(z[0], l)[0], ef_lo, ALU.mult)
                            dve.tensor_tensor(k_up, halves(z[1], l)[1], eb_up, ALU.mult)
                            dve.tensor_tensor(q_up, halves(q, l)[1], ef_up, ALU.mult)
                            dve.tensor_tensor(q_lo, halves(q, l)[0], eb_lo, ALU.mult).then_inc(mixed, 1)
                        if d == FIRST_LEVEL + 8:
                            dve.wait_ge(grams, nine + LEVELS + 1)
                            dve.tensor_copy(S_off, side[0][:, (nine + LEVELS) % 2 * 512:(nine + LEVELS) % 2 * 512 + 512]
                                            .rearrange("p (b t) -> p b t", t=P)).then_inc(kept, 1)
                        if d == FIRST_LEVEL + 10:
                            dve.wait_ge(rec_rstd_ready, u + 1)
                            evacuated(dve, CHUNKS.index(("gate_c", u // 2, KT)))
                            for h in range(2):
                                for m in range(MT):
                                    i = h * MT + m
                                    part = gate[:, m, (j + h) * HD:(j + h + 1) * HD]
                                    ins = dve.scalar_tensor_tensor(out=part, in0=side[1][:, i * P:(i + 1) * P],
                                                                   scalar=rec_rstd[:, i:i + 1], in1=part,
                                                                   op0=ALU.mult, op1=ALU.mult)
                            ins.then_inc(rec_y, 1)
                    for u, s0 in enumerate(UNITS):
                        b = u % 2
                        m = unit(u)[2]
                        nh = 1 if u < A_UNITS else 4
                        if s == s0 + 1:
                            dve.wait_ge(scored, u + 1)
                            if u:
                                dve.wait_ge(probs_turned, u)
                            if u < A_UNITS:
                                v = scores[:, 0:A_COLS]
                                link(dve.tensor_tensor(v, side[0][:, 0:A_COLS], masks[:, m, 0:A_COLS], ALU.add))
                                link(dve.reduce_max(smax[:, b, 0:1], v, AX.X))
                            else:
                                v = scores.rearrange("p (i t) -> p i t", i=4)
                                kv = (u - A_UNITS) // MT
                                dve.tensor_copy(v[:, :, T], sink[:, 4 * kv:4 * kv + 4])
                                link(dve.tensor_tensor(v[:, :, 0:T], side[0][:, :].rearrange("p (i t) -> p i t", i=4),
                                                       masks[:, m:m + 1, A_COLS:MASK_COLS].broadcast_to([P, 4, T]), ALU.add))
                                link(dve.reduce_max(smax[:, b, :], v, AX.X))
                            dve.tensor_scalar(nmax[:, b, 0:nh], smax[:, b, 0:nh], -SCALE, None, ALU.mult).then_inc(masked, 1)
                        if s == s0 + 3:
                            dve.wait_ge(probs, u + 1)
                            link(dve.reciprocal(rden[:, b, 0:nh], dens[:, b, 0:nh]))
                            by_query = rstd_apart if u < A_UNITS else x_rstd
                            link(dve.tensor_scalar(rden[:, b, 0:nh], rden[:, b, 0:nh], by_query[:, m:m + 1], None, ALU.mult))
                        if s == s0 + 4:
                            dve.wait_ge(attended, u + 1)
                            for i in range(nh):
                                if u < A_UNITS:
                                    if u == 0:
                                        evacuated(dve, 2 * NG)
                                    h = u // MT
                                    part = gate_a[:, m, h * HD:(h + 1) * HD]
                                else:
                                    part = gate_b[:, (u - A_UNITS) // MT, m, i * HD:(i + 1) * HD]
                                ins = dve.scalar_tensor_tensor(out=part, in0=side[1][:, i * P:(i + 1) * P],
                                                               scalar=rden[:, b, i:i + 1], in1=part,
                                                               op0=ALU.mult, op1=ALU.mult)
                            ins.then_inc(normed, 1)
                    n = split_at(s)
                    if n is not None:
                        _, _, blocks, hi_, lo_, gain, ps = turns[n]
                        dve.wait_ge(branch_hi, n + 1)
                        src = ps.rearrange("p (i t) -> p i t", t=T)
                        if n == 0:
                            in_order = lambda v: v.rearrange("p i (t m) -> p i m t", m=MT)
                            for m in range(MT):
                                ins = dve.scalar_tensor_tensor(
                                    out=in_order(lo_)[:, :, m], in0=src[:, :, m * P:(m + 1) * P], scalar=0.5,
                                    in1=in_order(hi_.bitcast(F32))[:, :, m], op0=ALU.mult, op1=ALU.subtract)
                            ins.then_inc(branch_lo, 1)
                        elif gain is None:
                            dve.scalar_tensor_tensor(out=lo_, in0=src, scalar=0.5, in1=hi_.bitcast(F32), op0=ALU.mult,
                                                     op1=ALU.subtract).then_inc(branch_lo, 1)
                        else:
                            for i in range(blocks):
                                ins = dve.scalar_tensor_tensor(out=lo_[:, i], in0=src[:, i], scalar=gain[:, i:i + 1],
                                                               in1=hi_[:, i].bitcast(F32), op0=ALU.mult, op1=ALU.subtract)
                            ins.then_inc(branch_lo, 1)
                    c = ENDS.get(s - 1)
                    if c is not None and CHUNKS[c][0].startswith("z_"):
                        kind, j, _ = CHUNKS[c]
                        dve.wait_ge(pe_step, s)
                        evacuated(dve, c - 1)
                        dst = y[:, :, j * CW:(j + 1) * CW] if kind == "z_a" else stage[:, :, :]
                        dve.scalar_tensor_tensor(out=dst, in0=stage[:, :, :], scalar=1.0, in1=accv[c % 2], op0=ALU.add,
                                                 op1=ALU.mult).then_inc(gated, 1)
                        dve.wait_ge(gated, (c - CHUNKS.index(("merge_a", 0, KT)) + 1) // 2)
                        dve.nop().then_inc(acc_free[c % 2], 1)
                    c = ENDS.get(s - 2)
                    if c is not None:
                        kind, i, _ = CHUNKS[c]
                        if kind.startswith("rope"):
                            rope(c, 2 if kind == "rope_kv" else 4)
                        if kind.startswith("gate"):
                            dve.wait_ge(tanhed, SILUS.index(c) + 1)
                            dst = {"gate_a": lambda: gate_a, "gate_b": lambda: gate_b[:, i],
                                   "gate_c": lambda: gate_c[i]}[kind]()
                            dve.scalar_tensor_tensor(out=dst, in0=dst, scalar=1.0, in1=accv[c % 2], op0=ALU.add,
                                                     op1=ALU.mult).then_inc(acc_free[c % 2], 1)
                        if kind == "out":
                            dve.wait_ge(branch_turned, 8 + i)
                            if i == 0:
                                dve.wait_ge(x_landed, 80)
                            for m in range(MT):
                                dve.wait_ge(out_squared, 2 * i + m + 1)
                                if i == 3 and m == MT - 1:
                                    dve.tensor_reduce(sumsq, out_sq.rearrange("p (m j) -> p m j", m=MT), AX.X,
                                                      ALU.add).then_inc(out_summed, 1)
                                ins = dve.tensor_tensor(y[:, m, i * CW:(i + 1) * CW], accv[c % 2][:, m],
                                                        post_gain[:, i * CW:(i + 1) * CW], ALU.mult)
                            ins.then_inc(acc_free[c % 2], 1)
                    c = ENDS.get(s - 3)
                    if c in ROPED:
                        dve.wait_ge(roped, ROPED.index(c) + 1)
                        turn_chunk(c, range(16 if CHUNKS[c][0] == "rope_kv" else 8))
                    if ENDS.get(s - 4) in ROPED and CHUNKS[ENDS[s - 4]][0] != "rope_kv":
                        turn_chunk(ENDS[s - 4], range(8, 16))
                    for k in range(4):
                        plain = ENDS.get(s - 1 - k)
                        if plain in TURNED and plain not in ROPED:
                            dve.wait_ge(staged, TURNED.index(plain) + 1)
                            turn_chunk(plain, range(4 * k, 4 * k + 4))
                    for k in range(2):
                        n = TURN_AT.get(s - k)
                        if n in BY_BLOCKS:
                            if n == 0:
                                dve.wait_ge(normed, A_UNITS)
                            elif n <= 2:
                                dve.wait_ge(normed, A_UNITS + B_UNITS)
                            elif n <= 6:
                                dve.wait_ge(rec_y, n - 2)
                            else:
                                dve.wait_ge(summed, 4 + n - 6)
                            if n:
                                dve.wait_ge(branch_lo, n)
                            ins = turn_blocks(turns[n][-1].rearrange("p (h t) -> p h t", t=T), turns[n][1],
                                              range(8 * k, 8 * k + 8))
                            if k == 1:
                                ins.then_inc(branch_turned, 1)
                    c = ENDS.get(s - 5)
                    if c is not None and CHUNKS[c][0] == "c_q":
                        dve.wait_ge(tanhed, SILUS.index(c) + 1)
                        dst = cq[CHUNKS[c][1]]
                        dve.scalar_tensor_tensor(out=dst, in0=q_tanh, scalar=1.0, in1=dst, op0=ALU.add, op1=ALU.mult)
                dve.wait_ge(out_rstd, 1)
                evacuated(dve, len(CHUNKS) - 1)
                evacuated(dve, len(CHUNKS) - 2)
                for p in range(3):
                    for m in range(MT):
                        cols = slice(p * PIECE, (p + 1) * PIECE)
                        ins = dve.scalar_tensor_tensor(out=x_sb[:, m, cols], in0=y[:, m, cols], scalar=rstd[:, m:m + 1],
                                                       in1=x_sb[:, m, cols], op0=ALU.mult, op1=ALU.add)
                    ins.then_inc(x_new, 1)
                for b in range(2):
                    dve.wait_ge(first_hi_ready, b + 1)
                    split_x_lo(dve, b, xT_ready)

            @block.tensor
            def _(pe):
                def mm(out, a, b, start=True, stop=True):
                    return pe.matmul(out, a, b, start=start, stop=stop)

                def stream(s, between):
                    c, q = STEPS[s]
                    kind, i, k = CHUNKS[c]
                    tile = (lambda v, m: apart(v)[:, m]) if kind in ("gate_a", "v_a") else (lambda v, m: v[:, m * P:(m + 1) * P])
                    if q == 0 and c >= 2:
                        evacuated(pe, c - 2)
                    if c == 0 and q:
                        pe.wait_ge(xT_ready, 2 * q)
                    if kind[:2] == "z_" and i == 0 and q == 0:
                        pe.wait_ge(branch_lo, {"z_a": 1, "z_b": 3, "z_c": 7}[kind])
                    if kind == "out" and i == 0:
                        pe.wait_ge(branch_lo, 8 + q)
                    if s:
                        pe.wait_ge(hi_ready, s)
                    for t in range(QK):
                        w = w_hi[:, s % 2, t * CW:(t + 1) * CW]
                        for n, part in enumerate(lhs(c, QK * q + t)):
                            for m in range(MT):
                                mm(acc[c % 2][:, m * CW:(m + 1) * CW], tile(part, m), w,
                                   start=(q == 0 and t == 0 and n == 0), stop=False)
                    between()
                    if s:
                        pe.wait_ge(lo_dve, s)
                        pe.wait_ge(lo_pool, s)
                    for t in range(QK):
                        w = w_lo[:, s % LANDING, t * CW:(t + 1) * CW]
                        part = lhs(c, QK * q + t)[0]
                        for m in range(MT):
                            ins = mm(acc[c % 2][:, m * CW:(m + 1) * CW], tile(part, m), w, start=False,
                                     stop=(q == k // QK - 1 and t == QK - 1))
                    ins.then_inc(pe_step, 1)

                def level_grams(s):
                    for u in range(4):
                        l = s - 1 - REC[u] - FIRST_LEVEL
                        if not -1 <= l < LEVELS:
                            continue
                        q = rec_views(u)[0]
                        n = (LEVELS + 1) * u + l + 1
                        pe.wait_ge(mixed, n + 1)
                        if n >= 2:
                            pe.wait_ge(kept, n - 1)
                        if n == 0:
                            pe.wait_ge(branch_lo, 3)
                        dst = side[0][:, n % 2 * 512:n % 2 * 512 + 512]
                        for b in range(4):
                            h, st = divmod(b, 2)
                            tt = 1 - st if l == LEVELS - 1 else st
                            qq = q if l < 0 else EQ[:, 3]
                            ins = mm(dst[:, b * P:(b + 1) * P], EQ[:, 2, h * T + st * P:h * T + (st + 1) * P],
                                     qq[:, h * T + tt * P:h * T + (tt + 1) * P])
                        ins.then_inc(grams, 1)

                for s in range(NSTEPS):
                    stream(s, lambda: level_grams(s))
                    if s == APART_AT:
                        pe.wait_ge(x_rstd_ready, 1)
                        pe.wait_ge(sorter_ready, 1)
                        for m in range(MT):
                            ins = mm(side[1][:, 4 * m:4 * m + 4], wide[:, m * P:(m + 1) * P], small[:, 22:26])
                        ins.then_inc(rstd_sorted, 1)
                    for u, s0 in enumerate(UNITS):
                        q, k, m = unit(u)
                        if s == s0:
                            if u == 0:
                                pe.wait_ge(turned, 2 * NG)
                            elif u == A_UNITS:
                                pe.wait_ge(turned, len(ROPED))
                                pe.wait_ge(branch_lo, 1)
                            if u:
                                pe.wait_ge(masked, u)
                            for i in range(len(q)):
                                if u >= A_UNITS:
                                    out = side[0][:, i * T:(i + 1) * T]
                                elif i == 0:
                                    out = side[0][:, 0:T].rearrange("p (m t) -> p m t", m=MT)
                                else:
                                    out = side[0][:, T + (i - 1) * P:T + i * P]
                                ins = mm(out, q[i], k[i])
                            ins.then_inc(scored, 1)
                        if s == s0 + 2:
                            pe.wait_ge(probs, u + 1)
                            if u:
                                pe.wait_ge(normed, u)
                            for n, (at, _, _) in enumerate(key_tiles(u)):
                                ins = pe.transpose(side[1][:, n * P:(n + 1) * P], scores[:, at:at + P], ident)
                            ins.then_inc(probs_turned, 1)
                        if s == s0 + 3:
                            pe.wait_ge(probs_copied, u + 1)
                            if u == 0:
                                for g in range(NG):
                                    evacuated(pe, 1 + 2 * NG + g)
                            tiles_ = key_tiles(u)
                            for n, (_, i, t) in enumerate(tiles_):
                                w = probsT[:, n * P:(n + 1) * P]
                                if u < A_UNITS:
                                    h = u // MT
                                    ins = mm(side[1][:, 0:P], w, va[:, i, t, h * HD:(h + 1) * HD],
                                             start=(n == 0), stop=(n == len(tiles_) - 1))
                                else:
                                    kv = (u - A_UNITS) // MT
                                    ins = mm(side[1][:, i * P:(i + 1) * P], w, vb[:, t, kv * HD:(kv + 1) * HD],
                                             start=(t == 0), stop=(t == MT - 1))
                            ins.then_inc(attended, 1)
                    for u in range(4):
                        d = s - REC[u]
                        _, _, v, _, _, j = rec_views(u)
                        nine = (LEVELS + 1) * u
                        if d == FIRST_LEVEL + 8:
                            pe.wait_ge(kept, nine + LEVELS + 1)
                            evacuated(pe, CHUNKS.index(("c_v", u // 2, KT)))
                            if u:
                                pe.wait_ge(rec_y, u)
                            for h in range(2):
                                for tt in range(MT):
                                    i = h * MT + tt
                                    o = side[1][:, i * P:(i + 1) * P]
                                    mm(o, S_diag[:, i], v[:, tt, (j + h) * HD:(j + h + 1) * HD], stop=False)
                                    ins = mm(o, S_off[:, h * MT + 1 - tt], v[:, 1 - tt, (j + h) * HD:(j + h + 1) * HD],
                                             start=False)
                            ins.then_inc(rec_out, 1)
                    n = TURN_AT.get(s)
                    if n is not None and n not in BY_BLOCKS:
                        _, src, blocks, _, _, _, ps = turns[n]
                        pe.wait_ge(summed, 8)
                        pe.wait_ge(rec_y, 4)
                        for i in range(blocks):
                            for m in range(MT):
                                ins = pe.transpose(ps[:, i * T + m * P:i * T + (m + 1) * P],
                                                   src[:, m, i * P:(i + 1) * P], ident)
                        ins.then_inc(branch_turned, 1)
                for _ in range(36):
                    pe.transpose(side[0][:, 0:P], ident, ident)
                for p in range(4):
                    if p < 3:
                        pe.wait_ge(x_new, p + 1)
                    else:
                        pe.wait_ge(x_new_pool, 1)
                    turn_x(pe, p)

        with nc.Fori(0, DEPTH) as layer:
            with nc.Block() as block:
                layer_body(layer, block)
            counts_from_zero()

        with nc.Block() as block:
            @block.sync
            def _(sp):
                sp.wait_ge(x_stored, 64 * (DEPTH + 1))


def constants():
    pos = np.arange(T, dtype=np.float32)
    freq = np.float32(THETA) ** (-np.arange(0, ROT, 2, dtype=np.float32) / np.float32(ROT))
    ang = (pos[:, None] * freq[None, :]).astype(np.float32)
    cos, sin = np.cos(ang), np.sin(ang)
    by_tile = lambda v: v.reshape(MT, P, ROT).transpose(1, 0, 2).reshape(P, MT * ROT)
    const = np.concatenate([np.eye(P, dtype=np.float32), by_tile(np.concatenate([cos, cos], 1)),
                            by_tile(np.concatenate([-sin, sin], 1))], 1).astype(np.float32)
    i = np.arange(T)
    rel = np.abs(i[:, None] - i[None, :])
    allowed = [(rel % dil == 0) & (rel // dil <= window // (2 * dil)) for window, dil in GROUPS] + [rel <= BWIN]
    masks = [np.where(a, 0.0, NEG).astype(np.float32) for a in allowed]
    apart = np.concatenate([i[m::MT] for m in range(MT)])
    mask_rows = []
    for m in range(MT):
        rows = slice(m * P, (m + 1) * P)
        a = [v[apart][:, apart][rows] for v in masks[:NG]]
        mask_rows.append(np.concatenate([a[0]] + [v[:, rows] for v in a[1:]] + [masks[NG][rows]], 1))
    masks = np.concatenate(mask_rows, 1)
    p = np.arange(P)
    levels = [((p[:, None] >> (l + 1)) == (p[None, :] >> (l + 1))) & ((p[:, None] >> l) != (p[None, :] >> l))
              for l in range(LEVELS - 1)]
    lmasks = np.stack(levels, 1).astype(np.float32).reshape(P, -1)
    return const, np.ascontiguousarray(masks), np.ascontiguousarray(lmasks)


def tiles(w):
    k, n = w.shape
    return w.reshape(k // (P * QK), QK, P, n // CW, CW).transpose(3, 0, 2, 1, 4)


W_IN_ORDER = [0, 1, 2, 3, 4, 5, 9, 6, 7, 8, 13, 14, 10, 11, 12, 15, 17, 19, 21, 23, 16, 18, 20, 22, 24]


def stream_of(w_in, w_a, w_b, w_c, w_out):
    t = tiles(w_in)
    parts = [t[c] for c in W_IN_ORDER]
    for b, w in enumerate((w_a, w_b, w_c)):
        z = tiles(w)
        for j in range(4):
            parts += [t[25 + 4 * b + j], z[j]]
    parts += list(tiles(w_out))
    return np.concatenate(parts, 0).reshape(NSTEPS, P, TILE)


def kernel(x, pre_norm, post_norm, w_in, sink_logits, hgrn_lower_bounds, hgrn_norm, w_branch_a, w_branch_b,
           w_branch_c, w_out):
    import concourse.bacc as bacc
    from concourse.bass_utils import run_bass_kernel_spmd

    x, pre_norm, post_norm, w_in, sink_logits, hgrn_lower_bounds, hgrn_norm, w_branch_a, w_branch_b, w_branch_c, w_out = (
        np.asarray(a) for a in (x, pre_norm, post_norm, w_in, sink_logits, hgrn_lower_bounds, hgrn_norm, w_branch_a,
                                w_branch_b, w_branch_c, w_out))
    const, masks, lmasks = constants()
    by_channel = lambda v: v.reshape(-1, P).T
    sel = [np.full((P, 1), float(layer > 0), np.float32) for layer in range(DEPTH)]
    par = np.stack([np.concatenate(
        [by_channel(pre_norm[n]), by_channel(hgrn_norm[n]), np.broadcast_to(sink_logits[n], (P, BQ)),
         by_channel(hgrn_lower_bounds.reshape(-1)), sel[n]], 1) for n in [*range(DEPTH), DEPTH - 1]])
    weights = [stream_of(w_in[n], w_branch_a[n], w_branch_b[n], w_branch_c[n], w_out[n]) for n in range(DEPTH)]
    weights = np.concatenate([*weights, weights[0][:LANDING]])
    arrays = {"w_stream": weights, "x_in": x, "const_in": const, "masks_in": masks, "lmasks_in": lmasks,
              "params_in": np.ascontiguousarray(par), "post_in": post_norm}
    nc = bacc.Bacc("TRN2", target_bir_lowering=False, num_devices=1)
    aps = [nc.dram_tensor(n, a.shape, mybir.dt.from_np(a.dtype), kind="ExternalInput").ap() for n, a in arrays.items()]
    out = nc.dram_tensor("x_out", x.shape, F32, kind="ExternalOutput").ap()
    build(nc, *aps, out)
    r = run_bass_kernel_spmd(nc, [arrays], core_ids=[0])
    return r.results[0]["x_out"]
```
